# Optimizing a Trainium2 kernel written in Bass

```python
import math
import jax
import jax.numpy as jnp
from jax import lax
import numpy as np

D_MODEL = 1024
BATCH = 1
SEQ = 512
DEPTH = 1
DEC_BATCH = 1
DEC_SEQ = 32
PAST_LEN = 256

CHUNK = 64
REC_BLOCK = CHUNK // 4
HG_HEADS = 4
HG_DK = 128
HG_DV = 128
GDN_HEADS = 4
GDN_DK = 128
GDN_DV = 128
CONV_W = 4
D_FF = -(-(8 * D_MODEL) // (3 * 256)) * 256
N_MOD = 6
EPS = 1e-6
HG_QK = HG_HEADS * HG_DK
HG_V = HG_HEADS * HG_DV
GDN_QK = GDN_HEADS * GDN_DK
GDN_V = GDN_HEADS * GDN_DV
CONV_CH = 2 * GDN_QK + GDN_V
IN_SIZES = (HG_QK, HG_QK, HG_V, HG_V, GDN_QK, GDN_QK, GDN_V, GDN_HEADS, GDN_HEADS, GDN_V, D_MODEL, D_MODEL)
D_IN = 2 * HG_QK + 2 * HG_V + 2 * GDN_QK + 2 * GDN_V + 2 * GDN_HEADS + 2 * D_MODEL

kernel_name = "hybrid_hgrn2_gdn_streaming_step"

def rmsnorm(x, w):
    xf = x.astype(jnp.float32)
    y = xf * lax.rsqrt(jnp.mean(jnp.square(xf), axis=-1, keepdims=True) + EPS)
    return (y * w.astype(jnp.float32)).astype(x.dtype)

def l2norm(x):
    xf = x.astype(jnp.float32)
    return xf * lax.rsqrt(jnp.sum(jnp.square(xf), axis=-1, keepdims=True) + EPS)

def split_cols(a, sizes):
    out, start = [], 0
    for s in sizes:
        out.append(a[..., start:start + s])
        start += s
    return out

def to_blocks(a, n_blocks):
    B, T = a.shape[:2]
    pad = [(0, 0), (0, n_blocks * REC_BLOCK - T)] + [(0, 0)] * (a.ndim - 2)
    a = jnp.pad(a, pad).reshape((B, n_blocks, REC_BLOCK) + a.shape[2:])
    return jnp.moveaxis(a, (1, 3), (0, 2))

def from_blocks(o, T):
    n, B, H, L, d = o.shape
    return o.transpose(1, 0, 3, 2, 4).reshape(B, n * L, H, d)[:, :T]

def chunk_gla(q, k, v, log_f, s0):
    T = q.shape[1]
    n = -(-T // REC_BLOCK)
    incl = jnp.tril(jnp.ones((REC_BLOCK, REC_BLOCK), dtype=bool))
    blocks = tuple(to_blocks(a.astype(jnp.float32), n) for a in (q, k, v, log_f))

    def step(S, blk):
        qc, kc, vc, gc = blk
        G = jnp.cumsum(gc, axis=2)
        rel = jnp.exp(jnp.where(incl[:, :, None], G[:, :, :, None, :] - G[:, :, None, :, :], -jnp.inf))
        A = jnp.einsum("bhtd,bhsd,bhtsd->bhts", qc, kc, rel)
        o = jnp.einsum("bhtd,bhdv->bhtv", qc * jnp.exp(G), S) + jnp.einsum("bhts,bhsv->bhtv", A, vc)
        G_last = G[:, :, -1:, :]
        S = jnp.exp(G_last[:, :, 0, :, None]) * S + jnp.einsum("bhsd,bhsv->bhdv", kc * jnp.exp(G_last - G), vc)
        return S, o

    S, o = lax.scan(step, s0.astype(jnp.float32), blocks)
    return from_blocks(o, T), S

def chunk_gated_delta(q, k, v, log_a, beta, s0):
    T = q.shape[1]
    n = -(-T // REC_BLOCK)
    dv = v.shape[-1]
    incl = jnp.tril(jnp.ones((REC_BLOCK, REC_BLOCK), dtype=bool))
    strict = jnp.tril(jnp.ones((REC_BLOCK, REC_BLOCK), dtype=bool), -1)
    eye = jnp.eye(REC_BLOCK, dtype=jnp.float32)
    blocks = tuple(to_blocks(a.astype(jnp.float32), n) for a in (q, k, v, log_a, beta))

    def step(S, blk):
        qc, kc, vc, gc, bc = blk
        G = jnp.cumsum(gc, axis=-1)
        rel = jnp.exp(jnp.where(incl, G[..., :, None] - G[..., None, :], -jnp.inf))
        M = jnp.where(strict, bc[..., :, None] * rel * jnp.einsum("bhtd,bhsd->bhts", kc, kc), 0.0)
        rhs = jnp.concatenate([bc[..., None] * vc, (bc * jnp.exp(G))[..., None] * kc], axis=-1)
        sol = lax.linalg.triangular_solve(eye + M, rhs, left_side=True, lower=True, unit_diagonal=True)
        u = sol[..., :dv] - jnp.einsum("bhtd,bhdv->bhtv", sol[..., dv:], S)
        qk = jnp.einsum("bhtd,bhsd->bhts", qc, kc) * rel
        o = jnp.einsum("bhtd,bhdv->bhtv", qc * jnp.exp(G)[..., None], S) + jnp.einsum("bhts,bhsv->bhtv", qk, u)
        S = jnp.exp(G[..., -1])[..., None, None] * S + jnp.einsum(
            "bhsd,bhsv->bhdv", kc * jnp.exp(G[..., -1:] - G)[..., None], u)
        return S, o

    S, o = lax.scan(step, s0.astype(jnp.float32), blocks)
    return from_blocks(o, T), S

def causal_conv(u, buf, w):
    T = u.shape[1]
    ext = jnp.concatenate([buf.astype(u.dtype), u], axis=1)
    y = ext[:, 0:T] * w[0]
    for j in range(1, CONV_W):
        y = y + ext[:, j:j + T] * w[j]
    return jax.nn.silu(y), ext[:, -(CONV_W - 1):]

def mixer(h, lb, s_hg, s_gdn, s_conv, w_in, hg_norm, conv_w, a_log, dt_bias, gdn_norm, w_pa, w_pb, w_out):
    B, T, _ = h.shape
    proj = h @ w_in
    hq, hf, hi, hog, gq, gk, gv, ga, gb, gz, gate_a, gate_b = split_cols(proj, IN_SIZES)
    heads = lambda a, d: a.reshape(B, T, -1, d)

    hf = hf.astype(jnp.float32)
    lb = lb.astype(jnp.float32)
    log_f = jnp.logaddexp(jnp.log(lb), jnp.log1p(-lb) + jax.nn.log_sigmoid(hf))
    k_hg = (1.0 - lb) * jax.nn.sigmoid(-hf)
    o_hg, s_hg_new = chunk_gla(heads(hq.astype(jnp.float32), HG_DK) * HG_DK ** -0.5, heads(k_hg, HG_DK),
                               heads(hi, HG_DV), heads(log_f, HG_DK), s_hg)
    o_hg = rmsnorm(o_hg, hg_norm) * jax.nn.silu(heads(hog, HG_DV).astype(jnp.float32))

    conv_out, s_conv_new = causal_conv(jnp.concatenate([gq, gk, gv], axis=-1), s_conv, conv_w)
    cq, ck, cv = split_cols(conv_out, (GDN_QK, GDN_QK, GDN_V))
    q = l2norm(heads(cq, GDN_DK)) * GDN_DK ** -0.5
    k = l2norm(heads(ck, GDN_DK))
    v = heads(cv, GDN_DV)
    log_a = -jnp.exp(a_log.astype(jnp.float32)) * jax.nn.softplus(ga.astype(jnp.float32) + dt_bias.astype(jnp.float32))
    beta = jax.nn.sigmoid(gb.astype(jnp.float32))
    o_gdn, s_gdn_new = chunk_gated_delta(q, k, v, log_a, beta, s_gdn)
    o_gdn = rmsnorm(o_gdn, gdn_norm) * jax.nn.silu(heads(gz, GDN_DV).astype(jnp.float32))

    y_a = o_hg.reshape(B, T, HG_V).astype(h.dtype) @ w_pa
    y_b = o_gdn.reshape(B, T, GDN_V).astype(h.dtype) @ w_pb
    y = jax.nn.sigmoid(gate_a) * y_a + jax.nn.sigmoid(gate_b) * y_b
    return y @ w_out, s_hg_new, s_gdn_new, s_conv_new

def swiglu(h, w_up, w_down):
    gate, up = jnp.split(h @ w_up, 2, axis=-1)
    return (jax.nn.silu(gate) * up) @ w_down

def trunk(x, c, s_hg, s_gdn, s_conv, lbs, w_ada, b_ada, norm_mix, w_in, hg_norm, conv_w, gdn_a_log,
          gdn_dt_bias, gdn_norm, w_proj_a, w_proj_b, w_out, norm_ffn, w_up, w_down, final_norm):
    new_hg, new_gdn, new_conv = [], [], []
    for l in range(DEPTH):
        mod = jax.nn.silu(c) @ w_ada[l] + b_ada[l]
        sh1, sc1, g1, sh2, sc2, g2 = [m[:, None, :] for m in jnp.split(mod, N_MOD, axis=-1)]
        h = rmsnorm(x, norm_mix[l]) * (1.0 + sc1) + sh1
        y, hg, gd, cv = mixer(h, lbs[l], s_hg[l], s_gdn[l], s_conv[l], w_in[l], hg_norm[l], conv_w[l],
                              gdn_a_log[l], gdn_dt_bias[l], gdn_norm[l], w_proj_a[l], w_proj_b[l], w_out[l])
        x = x + g1 * y
        h = rmsnorm(x, norm_ffn[l]) * (1.0 + sc2) + sh2
        x = x + g2 * swiglu(h, w_up[l], w_down[l])
        new_hg.append(hg)
        new_gdn.append(gd)
        new_conv.append(cv)
    return rmsnorm(x, final_norm), jnp.stack(new_hg), jnp.stack(new_gdn), jnp.stack(new_conv)

def setup_inputs(seed: int = 0) -> dict:
    key = jax.random.key(seed)
    ks = jax.random.split(key, 24)
    nrm = lambda k, shape, scale: jax.random.normal(k, shape, jnp.float32) * scale
    dt = jnp.exp(jax.random.uniform(ks[15], (DEPTH, GDN_HEADS), jnp.float32, math.log(1e-3), math.log(1e-1)))
    return {
        "x_prompt": nrm(ks[0], (BATCH, SEQ, D_MODEL), 1.0),
        "x_sample": nrm(ks[1], (DEC_BATCH, DEC_SEQ, D_MODEL), 1.0),
        "state_hgrn": nrm(ks[2], (DEPTH, DEC_BATCH, HG_HEADS, HG_DK, HG_DV), 0.5),
        "state_gdn": nrm(ks[3], (DEPTH, DEC_BATCH, GDN_HEADS, GDN_DK, GDN_DV), 0.1),
        "state_conv": nrm(ks[4], (DEPTH, DEC_BATCH, CONV_W - 1, CONV_CH), 1.0),
        "c_prompt": nrm(ks[5], (BATCH, D_MODEL), 1.0),
        "c_sample": nrm(ks[6], (DEC_BATCH, D_MODEL), 1.0),
        "w_ada": nrm(ks[7], (DEPTH, D_MODEL, N_MOD * D_MODEL), 0.5 * D_MODEL ** -0.5),
        "b_ada": nrm(ks[8], (DEPTH, N_MOD * D_MODEL), 0.02),
        "norm_mix": 1.0 + nrm(ks[9], (DEPTH, D_MODEL), 0.02),
        "w_in": nrm(ks[10], (DEPTH, D_MODEL, D_IN), D_MODEL ** -0.5),
        "hg_lb": nrm(ks[11], (DEPTH, HG_QK), 1.0),
        "hg_norm": 1.0 + nrm(ks[12], (DEPTH, HG_DV), 0.02),
        "conv_w": nrm(ks[13], (DEPTH, CONV_W, CONV_CH), CONV_W ** -0.5),
        "gdn_a_log": jnp.log(jax.random.uniform(ks[14], (DEPTH, GDN_HEADS), jnp.float32, 1.0, 16.0)),
        "gdn_dt_bias": dt + jnp.log(-jnp.expm1(-dt)),
        "gdn_norm": 1.0 + nrm(ks[16], (DEPTH, GDN_DV), 0.02),
        "w_proj_a": nrm(ks[17], (DEPTH, HG_V, D_MODEL), HG_V ** -0.5),
        "w_proj_b": nrm(ks[18], (DEPTH, GDN_V, D_MODEL), GDN_V ** -0.5),
        "w_out": nrm(ks[19], (DEPTH, D_MODEL, D_MODEL), D_MODEL ** -0.5),
        "norm_ffn": 1.0 + nrm(ks[20], (DEPTH, D_MODEL), 0.02),
        "w_up": nrm(ks[21], (DEPTH, D_MODEL, 2 * D_FF), D_MODEL ** -0.5),
        "w_down": nrm(ks[22], (DEPTH, D_FF, D_MODEL), D_FF ** -0.5),
        "final_norm": 1.0 + nrm(ks[23], (D_MODEL,), 0.02),
    }

def reference(x_prompt, x_sample, state_hgrn, state_gdn, state_conv, c_prompt, c_sample, w_ada, b_ada,
              norm_mix, w_in, hg_lb, hg_norm, conv_w, gdn_a_log, gdn_dt_bias, gdn_norm, w_proj_a, w_proj_b,
              w_out, norm_ffn, w_up, w_down, final_norm):
    lbs = jnp.cumsum(jax.nn.softmax(hg_lb.astype(jnp.float32), axis=0), axis=0)
    lbs = lbs - lbs[0:1]
    weights = (w_ada, b_ada, norm_mix, w_in, hg_norm, conv_w, gdn_a_log, gdn_dt_bias, gdn_norm,
               w_proj_a, w_proj_b, w_out, norm_ffn, w_up, w_down, final_norm)

    B = x_prompt.shape[0]
    zero_hg = jnp.zeros((DEPTH, B, HG_HEADS, HG_DK, HG_DV), jnp.float32)
    zero_gdn = jnp.zeros((DEPTH, B, GDN_HEADS, GDN_DK, GDN_DV), jnp.float32)
    zero_conv = jnp.zeros((DEPTH, B, CONV_W - 1, CONV_CH), x_prompt.dtype)
    y_prompt, hg_p, gdn_p, conv_p = trunk(x_prompt, c_prompt, zero_hg, zero_gdn, zero_conv, lbs, *weights)

    y_sample, hg_s, gdn_s, conv_s = trunk(x_sample, c_sample, state_hgrn, state_gdn, state_conv, lbs, *weights)

    return (y_prompt, y_sample, hg_p, gdn_p, conv_p, hg_s, gdn_s, conv_s)


_drawn_inputs = setup_inputs


def setup_inputs(seed=0):
    import zlib

    import numpy as np

    out = dict(_drawn_inputs(seed))
    spreads = {}
    factors = {'state_hgrn': 4.965, 'hg_norm': 8.0, 'gdn_norm': 8.0, 'norm_ffn': 8.0, 'final_norm': 2.903}
    for name, (base, spread) in spreads.items():
        noise = np.random.default_rng([zlib.crc32(name.encode()), seed]).standard_normal(out[name].shape)
        drawn = base * np.exp(spread * noise) if base else spread * noise
        out[name] = jnp.asarray(drawn.astype(out[name].dtype))
    for name, factor in factors.items():
        out[name] = (out[name] * factor).astype(out[name].dtype)
    return out
```

```python
from contextlib import ExitStack

import numpy as np

import concourse.bass as bass
from concourse import mybir

F32 = mybir.dt.float32
F32R = mybir.dt.float32r
U32 = mybir.dt.uint32
ALU = mybir.AluOpType
ACT = mybir.ActivationFunctionType

P = 128
D = 1024
KD = D // P
SEQ, DEC = 512, 32
TOK = SEQ + DEC
HALF = TOK // 2
NH = 4
CONV_W = 4
D_FF = 2816
KF = D_FF // P
EPS = 1e-6
LEVELS = 7
N_CHUNK = SEQ // P
CHUNKS = N_CHUNK + 1
FILLS = [(0, 1), (2, 3), (4,)]
QSCALE = float(P) ** -0.5
COL = dict(hq=0, hf=512, hi=1024, hog=1536, gq=2048, gk=2560, gv=3072, gagb=3584, gz=3592,
           gate_a=4104, gate_b=5128)
EXT = CONV_W - 1 + SEQ + CONV_W - 1 + DEC
CO = EXT - (CONV_W - 1)
SMP = SEQ + CONV_W - 1
VA = dict(b_ada=0, conv_w=48)
VB = dict(norm_mix=0, norm_ffn=8, final=16, hg=24, gdn=25, c=26, conv_state=42)
NA, NB = 96, 78


def length(c):
    return P if c < N_CHUNK else DEC


class Job:

    def __init__(self, w, nk, src, k0, group, first, last, m=P, col=0, pieces=None):
        self.w, self.nk, self.src, self.k0, self.group = w, nk, src, k0, group
        self.first, self.last, self.m, self.col, self.pieces = first, last, m, col, pieces


def make_plan(t):
    jobs, groups, plan = [], [], []

    def tile(w, c0, m=P):
        return w[:, c0:c0 + m].rearrange("(k p) m -> p k m", p=P)

    def add(kind, arg, parts):
        g = len(groups)
        for n, part in enumerate(parts):
            plan.append(("job", len(jobs)))
            jobs.append(Job(group=g, first=(n == 0), last=(n == len(parts) - 1), **part))
        groups.append((kind, arg, len(jobs) - 1))
        plan.append(("evac", g))

    def ada(v):
        add("ada", v, [dict(w=tile(t["w_ada"], v * D + n * P), nk=KD, src="c", k0=0, col=2 * n)
                       for n in range(KD)])

    def proj(kind, arg, c0):
        add(kind, arg, [dict(w=tile(t["w_in"], c0), nk=KD, src="h", k0=0)])

    def do(name, *arg):
        plan.append((name, *arg))

    def gdn_inputs(pair):
        for name, slot in (("gk", 2), ("gq", 0), ("gv", 4)):
            for h in range(2):
                proj("conv", (name, pair, h, slot + h), COL[name] + (2 * pair + h) * P)

    def hg_inputs(pair):
        for name in ("hi", "hq"):
            for h in range(2):
                proj(name, (pair, h), COL[name] + (2 * pair + h) * P)
            if name == "hi":
                do("h_v", pair)
        for h in range(2):
            proj("hf", (pair, h), COL["hf"] + (2 * pair + h) * P)

    do("vectors")
    do("x_in")
    do("sums")
    ada(0)
    ada(1)
    do("h1")
    add("gagb", 0, [dict(w=None, pieces=[(t["w_in"][:, 3584:3588].rearrange("(k p) m -> p k m", p=P), 0),
                                         (t["w_in"][:, 3588:3592].rearrange("(k p) m -> p k m", p=P), 32)],
                         nk=KD, src="h", k0=0, m=36)])
    do("g_rows")

    def gdn_steps(pair):
        s = [("g_norm", pair), ("g_bcast", pair), ("g_gram", pair), ("g_tok", pair)]
        for lv in range(LEVELS):
            s.append(("g_x", pair, lv))
            if lv:
                s.append(("g_y", pair, lv))
        s.append(("g_w", pair))
        for c in (0, 4, 1, 2, 3):
            s += [("g_u", pair, c), ("g_o", pair, c)]
        s.append(("g_end", pair))
        return s

    def hg_steps(pair):
        s = ([("conv_out",)] if pair == 0 else []) + [("h_diag", pair)]
        s += [("h_level", pair, lv) for lv in range(LEVELS)]
        s.append(("h_k", pair))
        s += [("h_o", pair, c) for c in (0, 4, 1, 2, 3)]
        s.append(("h_end", pair))
        return s

    def with_fillers(steps, start):
        own = plan[start:]
        del plan[start:]
        evacs = sum(x[0] == "evac" for x in own)
        per = -(-len(steps) // max(evacs, 1))
        left = list(steps)
        for x in own:
            plan.append(x)
            if x[0] == "evac":
                plan.extend(left[:per])
                del left[:per]
        plan.extend(left)

    gdn_inputs(0)
    at = len(plan)
    gdn_inputs(1)
    with_fillers(gdn_steps(0), at)
    at = len(plan)
    hg_inputs(0)
    with_fillers(gdn_steps(1), at)
    at = len(plan)
    hg_inputs(1)
    with_fillers(hg_steps(0), at)
    at = len(plan)
    for v in (2, 3, 4, 5):
        ada(v)
    with_fillers(hg_steps(1), at)
    for n in range(NH):
        proj("og", n, COL["hog"] + n * P)
        do("onorm", n)
    for n in range(NH):
        proj("og", NH + n, COL["gz"] + n * P)
        do("onorm", NH + n)
    do("x_load")
    do("x_in")
    for m in range(KD):
        proj("gate", ("a", m), COL["gate_a"] + m * P)
        add("pa", m, [dict(w=tile(t["w_pa"], m * P), nk=NH, src="o", k0=0)])
        proj("gate", ("b", m), COL["gate_b"] + m * P)
        add("pb", m, [dict(w=tile(t["w_pb"], m * P), nk=NH, src="o", k0=NH)])
    for m in range(KD):
        add("out", m, [dict(w=tile(t["w_out"], m * P), nk=KD, src="y", k0=0)])
    do("sums")
    do("h2")
    for m in range(KF):
        add("ffg", m, [dict(w=tile(t["w_up"], m * P), nk=KD, src="h2", k0=0)])
        add("ffu", m, [dict(w=tile(t["w_up"], D_FF + m * P), nk=KD, src="h2", k0=0)])
    for m in range(KD):
        parts = []
        for k0 in range(0, KF, KD):
            nk = min(KD, KF - k0)
            parts.append(dict(w=t["w_down"][k0 * P:(k0 + nk) * P, m * P:(m + 1) * P]
                              .rearrange("(k p) m -> p k m", p=P), nk=nk, src="a", k0=k0))
        add("down", m, parts)
    do("sums")
    do("y_out")
    return jobs, groups, plan


def bank_users(step):
    name, a = step[0], step[1:]
    n = len(FILLS)
    short = n if name not in ("g_x", "g_y", "h_level") or a[1] < 5 else n - 1
    return {
        "vectors": ["dve"] * 2, "x_in": ["act"] * (KD + 1), "sums": ["act"] * 2, "onorm": ["act"] * 2,
        "g_rows": ["dve"], "g_norm": ["act"] * 8, "g_bcast": ["act"] * n, "g_gram": ["dve"] * (2 * n),
        "g_tok": ["act"] * n + ["dve"] * (2 * n),
        "g_x": ["dve" if name == "g_x" and a[1] == 0 else "act"] * short,
        "g_y": ["dve"] * (short if name == "g_y" and a[1] == LEVELS - 1 else 2 * short),
        "g_w": ["act"] * n, "g_u": ["dve"], "g_o": ["act", "dve"],
        "conv_out": ["act"], "h_v": ["act"] * n, "h_diag": ["dve"] * n, "h_level": ["dve"] * short,
        "h_k": ["act"] * n, "h_o": ["act", "dve"], "y_out": ["act"] * (2 * CHUNKS),
    }.get(name, [])


GROUP_USER = dict(ada="dve", gagb="dve", conv="act", hi="act", hq="act", hf="act", og="act",
                  gate="act", pa="dve", pb="dve", out="dve", ffg="act", ffu="dve", down="dve")


def build(nc, t, outs):
    jobs, groups, plan = make_plan(t)
    y_p, y_s, hg_p, gdn_p, conv_p, hg_s, gdn_s, conv_s = outs

    first_fill, freed, slot_freed = [], [], []
    count = dict(act=0, dve=0)
    for step in plan:
        first_fill.append(len(freed))
        for user in bank_users(step):
            count[user] += 1
            freed.append((user, count[user]))
    count = dict(act=0, dve=0)
    for kind, _, _ in groups:
        count[GROUP_USER[kind]] += 1
        slot_freed.append((GROUP_USER[kind], count[GROUP_USER[kind]]))
    split = [i for i, j in enumerate(jobs) if j.src != "c"]
    nth_split = {i: n for n, i in enumerate(split)}
    vals_before = dict(h=0, o=KD, y=2 * KD, h2=3 * KD, a=4 * KD)
    gdn_chunks = (0, 4, 1, 2, 3)

    def nth(at):
        return sum(s[0] == plan[at][0] for s in plan[:at])

    order = [nth(n) for n in range(len(plan))]
    units = [s for s in plan if s[0] in ("g_end", "h_end")]

    ctx = ExitStack()
    with ctx:
        def sb(name, shape, dt=F32):
            return ctx.enter_context(nc.sbuf_tensor(name, shape, dt))

        def sem(name):
            return ctx.enter_context(nc.semaphore(name))

        masks = sb("masks", [P, LEVELS + 1, P])
        ones = sb("ones", [P, P])
        sel = sb("sel", [NH, NH, P])
        ident = masks[:, LEVELS, :]
        vecs = sb("vecs", [P, 2, P])
        vT = sb("vT", [P, NA + NB])
        cT = sb("cT", [P, 2, KD])
        mod = sb("mod", [P, 6 * KD, 2])
        gain = sb("gain", [P, 2, KD])
        eps = sb("eps", [P, 1])
        raw = sb("raw", [P, 3, KD, P])
        w_hi = sb("w_hi", [P, 2, KD, P], F32R)
        w_lo = sb("w_lo", [P, 2, KD, P], F32R)
        h_hi = sb("h_hi", [P, KD, TOK], F32R)
        h_lo = sb("h_lo", [P, KD, TOK], F32R)
        rn = sb("rn", [P, 2, TOK])
        sq = sb("sq", [P, 2, TOK])
        acc = sb("acc", [P, TOK])
        val = sb("val", [P, 2, TOK])
        base = (nc.sbuf_base + 31) // 32 * 32

        room = 229344 - base
        where = dict(rec=base, mix=base, ffn=base)

        def at(phase, name, shape, dt=F32, off=None):
            if off is None:
                off = where[phase]
                where[phase] = off + (int(np.prod(shape[1:])) * 4 + 31) // 32 * 32
                assert where[phase] <= base + room, (phase, name, where[phase] - base, room)
            return nc.alloc_sbuf_tensor_at(name, shape, dt, offset=off)

        row, tile = TOK * 4, CHUNKS * 2 * P * 4
        xT = at("rec", "xT", [P, KD, TOK])
        o = at("rec", "o", [P, 2 * NH, TOK])
        rows = at("rec", "rows", [NH, 4, TOK], off=base + KD * row)
        xtok = at("rec", "xtok", [P, CHUNKS, D], off=base + 36 * row)
        inp = at("rec", "inp", [P, 2, 6, TOK])
        ext = at("rec", "ext", [P, EXT])
        cy = at("rec", "cy", [P, CO])
        conv_keep = at("rec", "conv_keep", [P, 2, CONV_W - 1, 12])
        conv_rows = at("rec", "conv_rows", [2 * 12 * (CONV_W - 1), P])
        vec4 = at("rec", "vec4", [NH, 4])
        cols = at("rec", "cols", [P, CHUNKS, 2, NH])
        v_tok = at("rec", "v_tok", [P, 2, CHUNKS, 2, P])
        S = at("rec", "S", [P, 3, 2, P])
        relT = at("rec", "relT", [P, CHUNKS, 2, P])
        N = at("rec", "N", [P, CHUNKS, 2, P], off=base + 0 * tile)
        PT = at("rec", "PT", [P, CHUNKS, 2, P], off=base + 1 * tile)
        Tm = at("rec", "Tm", [P, CHUNKS, 2, P], off=base + 2 * tile)
        Um = at("rec", "Um", [P, CHUNKS, 2, P])
        X = at("rec", "X", [P, CHUNKS, 2, P])
        Wn = X
        Nl = at("rec", "Nl", [P, CHUNKS, 2, P])
        abc = at("rec", "abc", [P, 2, TOK], off=where["rec"] - CHUNKS * 2 * P * 4)
        kPG = at("rec", "kPG", [P, CHUNKS, 2, P])
        kD = at("rec", "kD", [P, CHUNKS, 2, P])
        u_tok = at("rec", "u_tok", [P, 2, P])
        elast = at("rec", "elast", [P, CHUNKS, 2])

        where["mix"] += 2 * KD * row
        o_hi = at("mix", "o_hi", [P, 2 * NH, TOK], F32R)
        o_lo = at("mix", "o_lo", [P, 2 * NH, TOK], F32R)
        gate = at("mix", "gate", [P, 2, TOK])
        ya = at("mix", "ya", [P, 2, TOK])
        assert where["mix"] == base + 36 * row
        y_hi = at("mix", "y_hi", [P, KD, TOK], F32R)
        y_lo = at("mix", "y_lo", [P, KD, TOK], F32R, off=base + KD * row)
        where["ffn"] += (KD + 2) * row
        a_hi = at("ffn", "a_hi", [P, KF, TOK], F32R)
        a_lo = at("ffn", "a_lo", [P, KF, TOK], F32R)
        g_act = at("ffn", "g_act", [P, 2, TOK], off=base + KD * row)
        ytok = at("ffn", "ytok", [P, 2, D], off=base + 16 * row)
        src = dict(h=(h_hi, h_lo), o=(o_hi, o_lo), y=(y_hi, y_lo), h2=(h_hi, h_lo), a=(a_hi, a_lo))

        G = ctx.enter_context(nc.psum_tensor("G", [P, 2, 2, 512], F32))
        R = ctx.enter_context(nc.psum_tensor("R", [P, 4, 512], F32))

        const_in = sem("const_in")
        vec_in = sem("vec_in")
        x_in = sem("x_in")
        w_in = [sem(f"w_in{n}") for n in range(3)]
        w_hi_done = sem("w_hi_done")
        w_lo_done = sem("w_lo_done")
        job_done = sem("job_done")
        slot_user = dict(act=sem("slot_read_act"), dve=sem("slot_read_dve"))
        fill_done = sem("fill_done")
        bank_user = dict(act=sem("bank_read_act"), dve=sem("bank_read_dve"))
        eps_set = sem("eps_set")
        c_sig = sem("c_sig")
        acc_ready = sem("acc_ready")
        sq_ready = sem("sq_ready")
        rn_ready = sem("rn_ready")
        rn_used = sem("rn_used")
        val_ready = sem("val_ready")
        hi_ready = sem("hi_ready")
        lo_ready = sem("lo_ready")
        dve_step = sem("dve_step")
        act_step = sem("act_step")
        ext_ready = sem("ext_ready")
        cy_ready = sem("cy_ready")
        conv_ready = sem("conv_ready")
        hist_zero = sem("hist_zero")
        x_rows = sem("x_rows")
        sp_log = sem("sp_log")
        sp_ready = sem("sp_ready")
        a_ready = sem("a_ready")
        pg_ready = sem("pg_ready")
        Nl_ready = sem("Nl_ready")
        U0_ready = sem("U0_ready")
        at_zero = sem("at_zero")
        hg_ready = sem("hg_ready")
        state_in = sem("state_in")
        state_out = sem("state_out")
        yT_ready = sem("yT_ready")
        y_out = [sem("y_out0"), sem("y_out1")]
        conv_sent = sem("conv_sent")

        def toks(c):
            return slice(c * P, c * P + length(c))

        def fill_view(bank, cs, square=True):
            L = length(cs[0])
            w = L if square else P
            return R[0:L if square is not None else P, bank, 0:len(cs) * 2 * w].rearrange(
                "p (c h t) -> p c h t", c=len(cs), h=2)

        def feat_view(bank, cs):
            L = length(cs[0])
            return R[:, bank, 0:len(cs) * 2 * L].rearrange("p (c h t) -> p c h t", c=len(cs), h=2)

        def heads_view(slots, cs):
            L = length(cs[0])
            return slots[:, :, cs[0] * P:cs[0] * P + len(cs) * L].rearrange("p h (c t) -> p c h t", t=L)

        def bc(ap, n):
            return ap.unsqueeze(len(ap.shape)).broadcast_to([*ap.shape, n])

        def mid(ap, n):
            return ap.unsqueeze(1).broadcast_to([ap.shape[0], n, ap.shape[1]])

        def slot_view(g):
            return G[:, g % 2, :, 0:HALF]

        def halves(ap):
            return ap.rearrange("p (n t) -> p n t", n=2)

        def wait_bank(eng, n):
            who, k = freed[n]
            eng.wait_ge(bank_user[who], k)

        def wait_slot(eng, g):
            who, k = slot_freed[g]
            eng.wait_ge(slot_user[who], k)

        def wait_group(eng, g):
            eng.wait_ge(job_done, groups[g][2] + 1)

        PIECES = [(0, 0, slice(0, HALF), slice(0, HALF)),
                  (0, 1, slice(0, SEQ - HALF), slice(HALF, SEQ)),
                  (1, 1, slice(SEQ - HALF, HALF), slice(SEQ, TOK))]
        GROUPS = [slice(0, SEQ), slice(SEQ, TOK)]
        norms = {}
        for n, s in enumerate(plan):
            norms[n] = sum(dict(sums=1, onorm=1, g_norm=4).get(x[0], 0) for x in plan[:n])
        head_norms = {n: sum(dict(onorm=1, g_norm=4).get(x[0], 0) for x in plan[:n]) for n in range(len(plan))}
        last_bank = {n: first_fill[n] + len(bank_users(s)) - 1 for n, s in enumerate(plan)}

        def spot(*step):
            return plan.index(step)

        def out_view(h0, c):
            return o[:, h0:h0 + 2, toks(c)]

        def copy_scores(dve, read, bank, n, lv):
            for k in range(len(bank_users(plan[n]))):
                cs = FILLS[k]
                b = bank(n, k)
                L = length(cs[0])
                for i, c in enumerate(cs):
                    ins = dve.copy_predicated(PT[0:L, c, :, 0:L], mid(masks[0:L, lv, 0:L].bitcast(U32), 2),
                                              fill_view(b, cs)[:, i])
                read(ins)

        def last_state(n):
            return last_bank[max(i for i in range(n) if plan[i][0] in ("g_o", "h_o"))]

        def unit(name, pair):
            return pair if name[0] == "g" else 2 + pair

        block = ctx.enter_context(nc.Block())

        @block.sync
        def _(sp):
            sp.dma_start(vecs[0:48, 0, :], t["b_ada"].rearrange("l (n p) -> (l n) p", p=P)).then_inc(vec_in, 16)
            sp.dma_start(vecs[48:96, 0, :], t["conv_w"].rearrange("l j (n p) -> (l j n) p", p=P)).then_inc(vec_in, 16)
            for name, key in (("norm_mix", "norm_mix"), ("norm_ffn", "norm_ffn")):
                r = VB[key]
                sp.dma_start(vecs[r:r + 8, 1, :], t[name].rearrange("l (n p) -> (l n) p", p=P)).then_inc(vec_in, 16)
            sp.dma_start(vecs[16:24, 1, :], t["final_norm"].rearrange("(n p) -> n p", p=P)).then_inc(vec_in, 16)
            sp.dma_start(vecs[24:25, 1, :], t["hg_norm"]).then_inc(vec_in, 16)
            sp.dma_start(vecs[25:26, 1, :], t["gdn_norm"]).then_inc(vec_in, 16)
            sp.dma_start(vecs[26:34, 1, :], t["c_prompt"].rearrange("l (n p) -> (l n) p", p=P)).then_inc(vec_in, 16)
            sp.dma_start(vecs[34:42, 1, :], t["c_sample"].rearrange("l (n p) -> (l n) p", p=P)).then_inc(vec_in, 16)
            sp.dma_start(vecs[42:78, 1, :], t["state_conv"].rearrange("l b j (n p) -> (l b j n) p", p=P)).then_inc(vec_in, 16)
            sp.dma_start(vec4[:, 0:1], t["gdn_dt_bias"].rearrange("l h -> h l")).then_inc(vec_in, 16)
            sp.dma_start(vec4[:, 1:2], t["gdn_a_log"].rearrange("l h -> h l")).then_inc(vec_in, 16)
            sp.dma_start(masks[:, :, :], t["level_masks"]).then_inc(const_in, 16)
            sp.dma_start(ones[:, :], t["all_ones"]).then_inc(const_in, 16)
            sp.dma_start(sel[:, :, :], t["head_select"]).then_inc(const_in, 16)
            sp.dma_start(xtok[:, 0:N_CHUNK, :], t["x_prompt"].rearrange("b (c p) d -> p (b c) d", p=P)).then_inc(x_in, 16)
            sp.dma_start(xtok[0:DEC, N_CHUNK, :], t["x_sample"].rearrange("b p d -> (b p) d")).then_inc(x_in, 16)
            for n, step in enumerate(plan):
                if step[0] == "x_load":
                    wait_bank(sp, last_bank[spot("h_o", 1, 3)])
                    sp.wait_ge(state_out, 32 * len(units))
                    sp.dma_start(xtok[:, 0:N_CHUNK, :], t["x_prompt"].rearrange("b (c p) d -> p (b c) d", p=P)).then_inc(x_in, 16)
                    sp.dma_start(xtok[0:DEC, N_CHUNK, :], t["x_sample"].rearrange("b p d -> (b p) d")).then_inc(x_in, 16)
                if step[0] == "job":
                    i = step[1]
                    if i >= 3:
                        if jobs[i - 3].src == "c":
                            sp.wait_ge(job_done, i - 2)
                        else:
                            sp.wait_ge(w_hi_done, nth_split[i - 3] + 1)
                            sp.wait_ge(w_lo_done, nth_split[i - 3] + 1)
                    job = jobs[i]
                    if job.pieces:
                        for piece, c0 in job.pieces:
                            sp.dma_start(raw[:, i % 3, 0:job.nk, c0:c0 + NH], piece).then_inc(w_in[i % 3], 16)
                    else:
                        sp.dma_start(raw[:, i % 3, 0:job.nk, 0:job.m], job.w).then_inc(w_in[i % 3], 16)
            for c in range(CHUNKS):
                L = length(c)
                wait_bank(sp, first_fill[spot("y_out")] + 2 * c + 1)
                dst = y_p[0, c * P:(c + 1) * P, :] if c < N_CHUNK else y_s[0]
                sp.dma_start(dst, ytok[0:L, c % 2, :]).then_inc(y_out[c % 2], 16)
            sp.wait_ge(y_out[0], 16 * 3)
            sp.wait_ge(y_out[1], 16 * 2)
            sp.wait_ge(conv_sent, 32)
            sp.wait_ge(state_out, 16 * 2 * len(units))

        landed = {}
        total = [0, 0, 0]
        for i, job in enumerate(jobs):
            total[i % 3] += 16 * (len(job.pieces) if job.pieces else 1)
            landed[i] = total[i % 3]

        def wait_weights(eng, i):
            eng.wait_ge(w_in[i % 3], landed[i])

        @block.gpsimd
        def _(pool):
            steps = 0

            def load_state(u):
                name = "state_gdn" if u < 2 else "state_hgrn"
                pair = u % 2
                pool.dma_start(S[:, 2, :, :], t[name][0, 0, 2 * pair:2 * pair + 2].rearrange("h d v -> d h v"))\
                    .then_inc(state_in, 16)

            for n, step in enumerate(plan):
                name = step[0]
                if name == "g_norm" and step[1] == 0:
                    pool.wait_ge(fill_done, last_bank[spot("x_in")] + 1)
                    load_state(0)
                if name == "g_x":
                    pair, lv = step[1:]
                    wait_bank(pool, first_fill[spot("g_gram", pair)] + 2)
                    if lv:
                        pool.wait_ge(fill_done, last_bank[spot("g_x", pair, lv - 1)] + 1)
                    if lv == 1:
                        pool.wait_ge(U0_ready, pair + 1)
                    if lv < 5:
                        pool.tensor_tensor(Nl[0:DEC, N_CHUNK, :, 0:DEC], N[0:DEC, N_CHUNK, :, 0:DEC],
                                           mid(masks[0:DEC, lv, 0:DEC], 2), ALU.mult)
                    pool.tensor_tensor(Nl[:, 0:N_CHUNK, :, :].rearrange("p c h t -> p (c h) t"),
                                       N[:, 0:N_CHUNK, :, :].rearrange("p c h t -> p (c h) t"),
                                       mid(masks[:, lv, :], 2 * N_CHUNK), ALU.mult).then_inc(Nl_ready, 1)
                    if lv == 0:
                        pool.wait_ge(Nl_ready, order[n] + 1)
                        pool.tensor_tensor(Um[0:DEC, N_CHUNK, :, 0:DEC], mid(ident[0:DEC, 0:DEC], 2),
                                           Nl[0:DEC, N_CHUNK, :, 0:DEC], ALU.subtract)
                        pool.tensor_tensor(Um[:, 0:N_CHUNK, :, :].rearrange("p c h t -> p (c h) t"),
                                           mid(ident, 2 * N_CHUNK),
                                           Nl[:, 0:N_CHUNK, :, :].rearrange("p c h t -> p (c h) t"),
                                           ALU.subtract).then_inc(U0_ready, 1)
                if name == "h_diag":
                    prev = units[unit(name, step[1]) - 1]
                    pool.wait_ge(fill_done, last_bank[plan.index(prev) - 1] + 1)
                    pool.memset(PT[:, :, :, :], 0.0).then_inc(at_zero, 1)
                if name == "conv_out":
                    wait_bank(pool, first_fill[n])
                    m = 12 * (CONV_W - 1)
                    for g, out in enumerate((conv_p, conv_s)):
                        pool.dma_start(out.rearrange("l b j (n p) -> (l b j n) p", p=P),
                                       conv_rows[g * m:(g + 1) * m, :]).then_inc(conv_sent, 16)
                if name in ("g_end", "h_end"):
                    u = unit(name, step[1])
                    pair = step[1]
                    wait_bank(pool, last_bank[n - 1])
                    for part, out in ((0, gdn_p if u < 2 else hg_p), (2, gdn_s if u < 2 else hg_s)):
                        pool.dma_start(out[0, 0, 2 * pair:2 * pair + 2].rearrange("h d v -> d h v"),
                                       S[:, part, :, :]).then_inc(state_out, 16)
                    if u + 1 < len(units):
                        pool.wait_ge(state_out, 32 * (u + 1))
                        load_state(u + 1)

        @block.scalar
        def _(act):
            fills = 0
            steps = [0]
            pend = []
            seen = dict(conv=0, gate=0, val=0, hg=0)

            def link(ins):
                steps[0] += 1
                ins.then_inc(act_step, 1)
                act.wait_ge(act_step, steps[0])

            def split_weights(i):
                if i >= len(jobs) or jobs[i].src == "c":
                    return
                m, job = nth_split[i], jobs[i]
                wait_weights(act, i)
                if m >= 2:
                    act.wait_ge(job_done, split[m - 2] + 1)
                act.activation(w_hi[:, m % 2, 0:job.nk, 0:job.m], raw[:, i % 3, 0:job.nk, 0:job.m],
                               ACT.Copy).then_inc(w_hi_done, 1)

            def split_val(dst, wait=True):
                v = seen["val"]
                seen["val"] += 1
                if wait:
                    act.wait_ge(val_ready, v + 1)
                act.activation(dst, val[:, v % 2, :], ACT.Copy).then_inc(hi_ready, 1)

            def conv_silu():
                if not pend:
                    return
                dst = pend.pop()
                act.wait_ge(cy_ready, seen["conv"])
                act.activation(dst[:, 0:SEQ], cy[:, 0:SEQ], ACT.Silu)
                act.activation(dst[:, SEQ:TOK], cy[:, SMP:SMP + DEC], ACT.Silu).then_inc(conv_ready, 1)

            def rnorm(q, bank, scale):
                dst = rn[:, q % 2, :]
                if q >= 2:
                    act.wait_ge(rn_used, q - 1)
                act.wait_ge(fill_done, bank + 1)
                act.activation(dst[:, 0:SEQ], R[:, bank % 4, 0:SEQ], ACT.Ln, bias=eps[:, 0:1], scale=scale)\
                    .then_inc(bank_user["act"], 1)
                act.wait_ge(fill_done, bank + 2)
                act.activation(dst[:, SEQ:TOK], R[:, (bank + 1) % 4, 0:DEC], ACT.Ln, bias=eps[:, 0:1],
                               scale=scale).then_inc(bank_user["act"], 1)
                wait_bank(act, bank + 1)
                act.activation(dst, dst, ACT.Exp, scale=-0.5).then_inc(rn_ready, 1)

            def read_banks(n, k0, pieces, func=ACT.Copy, scale=1.0):
                for k, (dst, view) in enumerate(pieces):
                    act.wait_ge(fill_done, first_fill[n] + k0 + k + 1)
                    act.activation(dst, view((first_fill[n] + k0 + k) % 4), func, scale=scale)\
                        .then_inc(bank_user["act"], 1)

            def chunk_pieces(dst, square, feat=False):
                out = []
                for cs in FILLS:
                    L = length(cs[0])
                    d = dst[0:P if feat else L, cs[0]:cs[-1] + 1, :, 0:L if (square or feat) else P]
                    out.append((d, (lambda b, cs=cs: feat_view(b, cs)) if feat
                                else (lambda b, cs=cs: fill_view(b, cs, square))))
                return out

            act.wait_ge(eps_set, 1)
            for n, step in enumerate(plan):
                name, a = step[0], step[1:]
                if name == "job":
                    split_weights(a[0] + 1)
                elif name == "vectors":
                    wait_bank(act, first_fill[n] + 1)
                    act.activation(cT[:, :, :], vT[:, NA + VB["c"]:NA + VB["c"] + 2 * KD]
                                   .rearrange("p (g k) -> p g k", g=2), ACT.Silu).then_inc(c_sig, 1)
                elif name == "x_in":
                    read_banks(n, 0, [(xT[:, k, 0:SEQ], lambda b: R[:, b, 0:SEQ]) for k in range(KD)])
                    read_banks(n, KD, [(xT[:, :, SEQ:TOK], lambda b: R[:, b, 0:KD * DEC]
                                        .rearrange("p (k t) -> p k t", k=KD))])
                elif name == "sums":
                    rnorm(norms[n], first_fill[n], 1.0 / D)
                elif name == "onorm":
                    rnorm(norms[n], first_fill[n], 1.0 / P)
                    split_val(o_hi[:, a[0], :])
                elif name in ("h1", "h2"):
                    for k in range(KD):
                        split_val(h_hi[:, k, :])
                elif name == "g_rows":
                    act.activation(vec4[:, 2:3], vec4[:, 1:2], ACT.Exp).then_inc(sp_log, 1)
                    act.wait_ge(x_rows, 1)
                    link(act.activation(rows[:, 1, :], rows[:, 1, :], ACT.Exp))
                    act.activation(rows[:, 1, :], rows[:, 1, :], ACT.Ln, bias=ones[0:NH, 0:1])
                    act.activation(rows[:, 2, :], rows[:, 2, :], ACT.Sigmoid).then_inc(sp_log, 1)
                    act.wait_ge(sp_ready, 1)
                    act.activation(rows[:, 0, :], rows[:, 0, :], ACT.Exp, scale=vec4[:, 3:4]).then_inc(a_ready, 1)
                elif name == "g_norm":
                    conv_silu()
                    for k in range(4):
                        rnorm(norms[n] + k, first_fill[n] + 2 * k, 1.0)
                elif name == "g_bcast":
                    read_banks(n, 0, [(abc[:, h, 0:SEQ], lambda b: R[:, b, 0:SEQ]) for h in range(2)])
                    read_banks(n, 2, [(abc[:, :, SEQ:TOK], lambda b: R[:, b, 0:2 * DEC]
                                       .rearrange("p (h t) -> p h t", h=2))])
                elif name in ("g_tok", "h_v"):
                    read_banks(n, 0, chunk_pieces(v_tok[:, a[0]], False))
                elif name == "g_x" and a[1]:
                    read_banks(n, 0, chunk_pieces(X, True)[:len(bank_users(step))])
                elif name == "g_w":
                    read_banks(n, 0, chunk_pieces(Wn, False, feat=True), scale=-1.0)
                elif name == "h_k":
                    read_banks(n, 0, chunk_pieces(kD, False))
                elif name in ("g_o", "h_o"):
                    h0 = (NH if name[0] == "g" else 0) + 2 * a[0]
                    c, L = a[1], length(a[1])
                    read_banks(n, 0, [(out_view(h0, c), lambda b: R[:, b, 0:2 * L].rearrange("p (h t) -> p h t", h=2))])
                elif name == "conv_out":
                    read_banks(n, 0, [(conv_rows[:, :], lambda b: R[0:72, b, 0:P])])
                elif name == "y_out":
                    for c in range(CHUNKS):
                        L = length(c)
                        if c >= 2:
                            act.wait_ge(y_out[c % 2], 16 * (c // 2))
                        for k in range(2):
                            b = first_fill[n] + 2 * c + k
                            act.wait_ge(fill_done, b + 1)
                            act.activation(ytok[0:L, c % 2, k * 512:(k + 1) * 512], R[0:L, b % 4, :], ACT.Copy)\
                                .then_inc(bank_user["act"], 1)
                elif name == "evac":
                    g = a[0]
                    kind, arg, _ = groups[g]
                    if kind == "conv":
                        what, pair, h, slot = arg
                        conv_silu()
                        c = seen["conv"]
                        seen["conv"] += 1
                        tile = dict(gq=0, gk=4, gv=8)[what] + 2 * pair + h
                        if c:
                            act.wait_ge(cy_ready, c)
                        else:
                            act.wait_ge(hist_zero, 1)
                        act.activation(ext[:, SEQ + 3:SEQ + 6], vT[:, NA + VB["conv_state"] + tile:
                                       NA + VB["conv_state"] + tile + 25:12], ACT.Copy)
                        wait_group(act, g)
                        s = g % 2
                        act.activation(ext[:, 3:3 + HALF], G[:, s, 0, 0:HALF], ACT.Copy)
                        act.activation(ext[:, 3 + HALF:3 + SEQ], G[:, s, 1, 0:SEQ - HALF], ACT.Copy)
                        act.activation(ext[:, SEQ + 6:EXT], G[:, s, 1, SEQ - HALF:HALF], ACT.Copy)\
                            .then_inc(slot_user["act"], 1)
                        wait_slot(act, g)
                        act.activation(conv_keep[:, 0, :, tile], ext[:, SEQ:SEQ + 3], ACT.Copy)
                        act.activation(conv_keep[:, 1, :, tile], ext[:, EXT - 3:EXT], ACT.Copy)\
                            .then_inc(ext_ready, 1)
                        pend.append(inp[:, pair, slot, :])
                    elif kind in ("hi", "hq"):
                        pair, h = arg
                        wait_group(act, g)
                        dst = inp[:, pair, (4 if kind == "hi" else 0) + h, :]
                        act.activation(halves(dst), slot_view(g), ACT.Copy,
                                       scale=QSCALE if kind == "hq" else 1.0).then_inc(slot_user["act"], 1)
                    elif kind == "hf":
                        pair, h = arg
                        wait_group(act, g)
                        act.activation(halves(inp[:, pair, 4 + h, :]), slot_view(g), ACT.Sigmoid)
                        act.activation(halves(inp[:, pair, 2 + h, :]), slot_view(g), ACT.Sigmoid, scale=-1.0)\
                            .then_inc(slot_user["act"], 1)
                    elif kind in ("og", "gate"):
                        c = seen["gate"]
                        seen["gate"] += 1
                        if c == 0:
                            act.wait_ge(conv_sent, 32)
                        if 2 <= c < 2 * NH + 2:
                            act.wait_ge(val_ready, vals_before["o"] + c - 1)
                        elif c >= 2:
                            wait_slot(act, g - 3)
                        wait_group(act, g)
                        act.activation(halves(gate[:, c % 2, :]), slot_view(g),
                                       ACT.Silu if kind == "og" else ACT.Sigmoid).then_inc(slot_user["act"], 1)
                    elif kind == "pb":
                        if arg == 0:
                            act.wait_ge(state_out, 32 * len(units))
                        split_val(y_hi[:, arg, :])
                    elif kind == "ffg":
                        wait_group(act, g)
                        if arg >= 2:
                            wait_slot(act, g - 3)
                        act.activation(halves(g_act[:, arg % 2, :]), slot_view(g), ACT.Silu)\
                            .then_inc(slot_user["act"], 1)
                    elif kind == "ffu":
                        wait_slot(act, g)
                        split_val(a_hi[:, arg, :], False)

        @block.vector
        def _(dve):
            steps = [0]
            later = []
            seen = dict(val=0, conv=0, gate=0, u=0, s=0)

            def link(ins):
                steps[0] += 1
                ins.then_inc(dve_step, 1)
                dve.wait_ge(dve_step, steps[0])

            def read(ins):
                ins.then_inc(bank_user["dve"], 1)

            def split_weights(i):
                if i >= len(jobs) or jobs[i].src == "c":
                    return
                m, job = nth_split[i], jobs[i]
                dve.wait_ge(w_hi_done, m + 1)
                at = (slice(None), m % 2, slice(0, job.nk), slice(0, job.m))
                dve.tensor_tensor(w_lo[at], raw[:, i % 3, 0:job.nk, 0:job.m], w_hi[at].bitcast(F32),
                                  ALU.subtract).then_inc(w_lo_done, 1)

            def low_parts():
                while later:
                    v, hi, lo = later.pop(0)
                    dve.wait_ge(hi_ready, v + 1)
                    dve.tensor_tensor(lo, val[:, v % 2, :], hi.bitcast(F32), ALU.subtract).then_inc(lo_ready, 1)

            def new_val(hi, lo):
                v = seen["val"]
                seen["val"] += 1
                low_parts()
                if v >= 2:
                    dve.wait_ge(lo_ready, v - 1)
                later.append((v, hi, lo))
                return val[:, v % 2, :]

            def bank(n, k):
                dve.wait_ge(fill_done, first_fill[n] + k + 1)
                return (first_fill[n] + k) % 4

            def add_square(m):
                if m == 0:
                    link(dve.tensor_tensor(acc[:, :], xT[:, 0, :], xT[:, 0, :], ALU.mult))
                else:
                    link(dve.tensor_tensor(sq[:, 0, :], xT[:, m, :], xT[:, m, :], ALU.mult))
                    ins = dve.tensor_tensor(acc[:, :], acc[:, :], sq[:, 0, :], ALU.add)
                    if m == KD - 1:
                        ins.then_inc(acc_ready, 1)
                    else:
                        link(ins)

            dve.memset(eps[:, :], EPS).then_inc(eps_set, 1)
            dve.memset(ext[:, 0:3], 0.0).then_inc(hist_zero, 1)
            for n, step in enumerate(plan):
                name, a = step[0], step[1:]
                if name == "job":
                    split_weights(a[0] + 1)
                    low_parts()
                elif name == "vectors":
                    b = bank(n, 0)
                    read(dve.tensor_copy(vT[:, 0:NA], R[:, b, 0:NA]))
                    b = bank(n, 1)
                    read(dve.tensor_copy(vT[:, NA:NA + NB], R[:, b, 0:NB]))
                    wait_bank(dve, first_fill[n] + 1)
                elif name == "x_in" and order[n] == 0:
                    for k in range(KD):
                        wait_bank(dve, first_fill[n] + KD)
                        add_square(k)
                elif name in ("h1", "h2"):
                    low_parts()
                    sh, sc, norm = (0, 1, "norm_mix") if name == "h1" else (3, 4, "norm_ffn")
                    for g in range(2):
                        link(dve.scalar_tensor_tensor(gain[:, g, :], mod[:, sc * KD:(sc + 1) * KD, g], 1.0,
                                                      vT[:, NA + VB[norm]:NA + VB[norm] + KD], ALU.add, ALU.mult))
                    q = norms[n] - 1
                    dve.wait_ge(rn_ready, q + 1)
                    for k in range(KD):
                        x = new_val(h_hi[:, k, :], h_lo[:, k, :])
                        ins = dve.tensor_tensor(x, xT[:, k, :], rn[:, q % 2, :], ALU.mult)
                        if k < KD - 1:
                            link(ins)
                        else:
                            ins.then_inc(rn_used, 1)
                            dve.wait_ge(rn_used, q + 1)
                        for g, cols_ in enumerate(GROUPS):
                            ins = dve.tensor_scalar(x[:, cols_], x[:, cols_], gain[:, g, k:k + 1],
                                                    mod[:, sh * KD + k, g:g + 1], ALU.mult, ALU.add)
                        ins.then_inc(val_ready, 1)
                    low_parts()
                elif name == "g_rows":
                    b = bank(n, 0)
                    for c0, c1, L in ((0, N_CHUNK, P), (N_CHUNK, CHUNKS, DEC)):
                        ins = dve.tensor_copy(cols[0:L, c0:c1, :, :].rearrange("p c k h -> p c (k h)"),
                                              R[0:L, b, 8 * c0:8 * c1].rearrange("p (c k) -> p c k", c=c1 - c0))
                    read(ins)
                    wait_bank(dve, first_fill[n])
                elif name == "g_norm":
                    pair = a[0]
                    q0, s0 = norms[n], head_norms[n]

                    def square(k):
                        x = inp[:, pair, k, :]
                        if k == 0:
                            dve.wait_ge(conv_ready, 6 * (pair + 1))
                        if s0 + k >= 2:
                            dve.wait_ge(rn_ready, q0 + k - 1)
                        dve.tensor_tensor(sq[:, (s0 + k) % 2, :], x, x, ALU.mult).then_inc(sq_ready, 1)

                    square(0)
                    square(1)
                    for k in range(4):
                        x = inp[:, pair, k, :]
                        dve.wait_ge(rn_ready, q0 + k + 1)
                        dve.scalar_tensor_tensor(x, x, QSCALE if k < 2 else 1.0, rn[:, (q0 + k) % 2, :],
                                                 ALU.mult, ALU.mult).then_inc(rn_used, 1)
                        if k + 2 < 4:
                            square(k + 2)
                elif name == "g_gram":
                    pair = a[0]
                    wait_bank(dve, last_bank[spot("g_bcast", pair)])
                    for c in range(CHUNKS):
                        L = length(c)
                        for h in range(2):
                            ins = dve.tensor_tensor_scan(relT[0:L, c, h, 0:L], abc[0:L, h, toks(c)],
                                                         ident[0:L, 0:L], 0.0, ALU.mult, ALU.add)
                    link(ins)
                    for k, cs in enumerate(FILLS):
                        b = bank(n, k)
                        L = length(cs[0])
                        for c in cs:
                            for h in range(2):
                                ins = dve.scalar_tensor_tensor(N[0:L, c, h, 0:L], relT[0:L, c, h, 0:L],
                                                               cols[0:L, c, 0, 2 * pair + h:2 * pair + h + 1],
                                                               fill_view(b, cs)[:, c - cs[0], h, :],
                                                               ALU.mult, ALU.mult)
                        read(ins)
                    for k, cs in enumerate(FILLS):
                        b = bank(n, 3 + k)
                        L = length(cs[0])
                        d = (slice(0, L), slice(cs[0], cs[-1] + 1), slice(None), slice(0, L))
                        read(dve.tensor_tensor(PT[d], relT[d], fill_view(b, cs), ALU.mult))
                elif name == "g_tok":
                    pair = a[0]
                    hs = slice(2 * pair, 2 * pair + 2)
                    for k, cs in enumerate(FILLS):
                        b = bank(n, 3 + k)
                        L, cc = length(cs[0]), slice(cs[0], cs[-1] + 1)
                        for i, c in enumerate(cs):
                            dve.tensor_tensor(kPG[0:L, c, :, :], fill_view(b, cs, False)[:, i], bc(cols[0:L, c, 1, hs], P),
                                              ALU.mult)
                            ins = dve.tensor_tensor(kD[0:L, c, :, :], fill_view(b, cs, False)[:, i],
                                                    bc(relT[0:L, c, :, L - 1], P), ALU.mult)
                        read(ins)
                    q = inp[:, pair, 0:2, :]
                    for h in range(2):
                        b = bank(n, 6 + h)
                        dve.tensor_copy(elast[:, 0:N_CHUNK, h], R[:, b, P - 1:SEQ:P])
                        read(dve.tensor_tensor(q[:, h, 0:SEQ], q[:, h, 0:SEQ], R[:, b, 0:SEQ], ALU.mult))
                    b = bank(n, 8)
                    v = R[:, b, 0:2 * DEC].rearrange("p (h t) -> p h t", h=2)
                    dve.tensor_copy(elast[:, N_CHUNK, :], v[:, :, DEC - 1])
                    read(dve.tensor_tensor(q[:, :, SEQ:TOK], q[:, :, SEQ:TOK], v, ALU.mult))
                elif name == "g_x" and a[1] == 0:
                    for k, cs in enumerate(FILLS):
                        b = bank(n, k)
                        L = length(cs[0])
                        for i, c in enumerate(cs):
                            ins = dve.tensor_tensor(Tm[0:L, c, :, 0:L], mid(ident[0:L, 0:L], 2), fill_view(b, cs)[:, i],
                                                    ALU.subtract)
                        read(ins)
                elif name == "g_y":
                    pair, lv = a
                    todo = FILLS if lv < 5 else FILLS[:2]
                    k = 0
                    if lv == 1:
                        dve.wait_ge(U0_ready, pair + 1)
                    for dst in ((Tm, Um) if lv < LEVELS - 1 else (Um,)):
                        for cs in todo:
                            b = bank(n, k)
                            L = length(cs[0])
                            d = (slice(0, L), slice(cs[0], cs[-1] + 1), slice(None), slice(0, L))
                            if k == 0:
                                wait_bank(dve, last_bank[spot("g_x", pair, 0) if lv == 1 else
                                                         spot("g_y", pair, lv - 1)])
                            read(dve.tensor_tensor(dst[d], dst[d], fill_view(b, cs), ALU.subtract))
                            k += 1
                elif name == "g_u":
                    pair, c = a
                    L = length(c)
                    b = bank(n, 0)
                    if seen["u"]:
                        dve.wait_ge(fill_done, last_bank[max(i for i in range(n) if plan[i][0] == "g_o")] + 1)
                    seen["u"] += 1
                    read(dve.tensor_tensor(u_tok[0:L, :, :], R[0:L, b, 0:2 * P].rearrange("p (h v) -> p h v", h=2),
                                           bc(cols[0:L, c, 0, 2 * pair:2 * pair + 2], P), ALU.mult))
                elif name in ("g_o", "h_o"):
                    pair, c = a
                    u = unit(name, pair)
                    b = bank(n, 1)
                    if seen["s"] % CHUNKS == 0 and u:
                        dve.wait_ge(state_out, 32 * u)
                    if c == N_CHUNK:
                        dve.wait_ge(state_in, 16 * (u + 1))
                    if seen["s"]:
                        wait_bank(dve, last_state(n))
                    old, new = (2, 2) if c == N_CHUNK else (c % 2, (c + 1) % 2)
                    for h in range(2):
                        new_s = R[:, b, h * P:(h + 1) * P]
                        if c == 0:
                            ins = dve.tensor_copy(S[:, new, h, :], new_s)
                        else:
                            last = (c + 1) * P - 1 if c < N_CHUNK else TOK - 1
                            decay = elast[:, c, h:h + 1] if name == "g_o" else inp[:, pair, 4 + h, last:last + 1]
                            ins = dve.scalar_tensor_tensor(S[:, new, h, :], S[:, old, h, :], decay, new_s,
                                                           ALU.mult, ALU.add)
                    read(ins)
                    seen["s"] += 1
                elif name == "h_diag":
                    dve.wait_ge(at_zero, a[0] + 1)
                    copy_scores(dve, read, bank, n, LEVELS)
                    q, f = inp[:, a[0], 0:2, :], inp[:, a[0], 4:6, :]
                    dve.wait_ge(slot_user["act"], slot_freed[max(g for g, x in enumerate(groups)
                                                             if x[0] == "hf" and x[1] == (a[0], 1))][1])
                    dve.tensor_tensor(q, q, f, ALU.mult).then_inc(hg_ready, 1)
                elif name == "h_level":
                    pair, lv = a
                    copy_scores(dve, read, bank, n, lv)
                    h = 1 << lv
                    end = TOK if lv < 5 else SEQ
                    q, k, f = (inp[:, pair, s:s + 2, 0:end].rearrange("p n (b x t) -> p n b x t", x=2, t=h)
                               for s in (0, 2, 4))
                    dve.wait_ge(hg_ready, order[n] + pair + 1)
                    for hd in range(2):
                        dve.tensor_tensor(q[:, hd, :, 1, :], q[:, hd, :, 1, :], bc(f[:, hd, :, 0, h - 1], h), ALU.mult)
                        ins = dve.tensor_tensor(k[:, hd, :, 0, :], k[:, hd, :, 0, :], bc(f[:, hd, :, 1, h - 1], h), ALU.mult)
                    link(ins)
                    dve.tensor_tensor(f[:, :, :, 1, h - 1], f[:, :, :, 1, h - 1], f[:, :, :, 0, h - 1],
                                      ALU.mult).then_inc(hg_ready, 1)
                elif name == "onorm":
                    hd = a[0]
                    low_parts()
                    q, s = norms[n], head_norms[n]
                    dve.wait_ge(rn_ready, q)
                    wait_bank(dve, last_bank[spot("h_o", 1, 3)] - 1)
                    dve.tensor_tensor(sq[:, s % 2, :], o[:, hd, :], o[:, hd, :], ALU.mult).then_inc(sq_ready, 1)
                    if hd == 0:
                        dve.wait_ge(conv_sent, 32)
                    x = new_val(o_hi[:, hd, :], o_lo[:, hd, :])
                    dve.wait_ge(rn_ready, q + 1)
                    w = NA + (VB["hg"] if hd < NH else VB["gdn"])
                    ins = dve.scalar_tensor_tensor(x, o[:, hd, :], vT[:, w:w + 1], rn[:, q % 2, :], ALU.mult, ALU.mult)
                    ins.then_inc(rn_used, 1)
                    dve.wait_ge(rn_used, q + 1)
                    c = seen["gate"]
                    seen["gate"] += 1
                    wait_slot(dve, max(g for g, z in enumerate(groups) if z[0] == "og" and z[1] == hd))
                    dve.tensor_tensor(x, x, gate[:, c % 2, :], ALU.mult).then_inc(val_ready, 1)
                elif name == "y_out":
                    q = norms[n] - 1
                    dve.wait_ge(rn_ready, q + 1)
                    for k in range(KD):
                        dve.scalar_tensor_tensor(xT[:, k, :], xT[:, k, :], vT[:, NA + VB["final"] + k:NA + VB["final"] + k + 1],
                                                 rn[:, q % 2, :], ALU.mult, ALU.mult).then_inc(yT_ready, 1)
                elif name == "evac":
                    g = a[0]
                    kind, arg, _ = groups[g]
                    s = g % 2
                    done = slot_user["dve"]
                    if kind == "ada":
                        wait_group(dve, g)
                        dve.tensor_tensor(mod[:, arg * KD:(arg + 1) * KD, :],
                                          G[:, s, 0, 0:2 * KD].rearrange("p (k g) -> p k g", g=2),
                                          bc(vT[:, arg * KD:(arg + 1) * KD], 2), ALU.add).then_inc(done, 1)
                        wait_slot(dve, g)
                    elif kind == "gagb":
                        wait_group(dve, g)
                        dve.wait_ge(sp_log, 1)
                        dve.tensor_scalar(vec4[:, 3:4], vec4[:, 2:3], -1.0, None, ALU.mult)
                        ga = G[0:NH, s, :, 0:HALF]
                        dve.tensor_scalar(halves(rows[:, 0, :]), ga, vec4[:, 0:1], 0.0, ALU.add, ALU.max)
                        dve.tensor_copy(halves(rows[:, 2, :]), G[32:32 + NH, s, :, 0:HALF])
                        dve.tensor_scalar(halves(rows[:, 1, :]), ga, vec4[:, 0:1], None, ALU.add).then_inc(done, 1)
                        wait_slot(dve, g)
                        dve.scalar_tensor_tensor(rows[:, 1, :], rows[:, 0, :], -2.0, rows[:, 1, :], ALU.mult,
                                                 ALU.add).then_inc(x_rows, 1)
                        dve.wait_ge(sp_log, 2)
                        dve.tensor_tensor(rows[:, 0, :], rows[:, 0, :], rows[:, 1, :], ALU.add).then_inc(sp_ready, 1)
                        dve.wait_ge(a_ready, 1)
                        for c in range(CHUNKS):
                            ins = dve.tensor_tensor_scan(rows[:, 3, toks(c)], rows[:, 0, toks(c)],
                                                         ones[0:NH, 0:length(c)], 1.0, ALU.mult, ALU.mult)
                        ins.then_inc(pg_ready, 1)
                    elif kind == "conv":
                        what, pair, h, slot = arg
                        c = seen["conv"]
                        seen["conv"] += 1
                        tile = dict(gq=0, gk=4, gv=8)[what] + 2 * pair + h
                        dve.wait_ge(ext_ready, c + 1)
                        if c:
                            dve.wait_ge(conv_ready, c)
                        w = [vT[:, 48 + j * 12 + tile:49 + j * 12 + tile] for j in range(CONV_W)]
                        link(dve.tensor_scalar(cy[:, :], ext[:, 0:CO], w[0], None, ALU.mult))
                        for j in range(1, CONV_W):
                            ins = dve.scalar_tensor_tensor(cy[:, :], ext[:, j:j + CO], w[j], cy[:, :], ALU.mult, ALU.add)
                            if j < CONV_W - 1:
                                link(ins)
                        ins.then_inc(cy_ready, 1)
                    elif kind == "gate" and arg[0] == "a":
                        pass
                    elif kind in ("pa", "pb"):
                        wait_group(dve, g)
                        gg = g - 1
                        wait_slot(dve, gg)
                        c = seen["gate"]
                        seen["gate"] += 1
                        k = 0 if kind == "pa" else 1
                        ins = dve.tensor_tensor(halves(ya[:, k, :]), slot_view(g), halves(gate[:, c % 2, :]), ALU.mult)
                        ins.then_inc(done, 1)
                        wait_slot(dve, g)
                        if kind == "pb":
                            x = new_val(y_hi[:, arg, :], y_lo[:, arg, :])
                            dve.tensor_tensor(x, ya[:, 0, :], ya[:, 1, :], ALU.add).then_inc(val_ready, 1)
                    elif kind in ("out", "down"):
                        wait_group(dve, g)
                        v = 2 if kind == "out" else 5
                        if kind == "out" and arg == 0:
                            wait_bank(dve, last_bank[len(plan) - 1 - plan[::-1].index(("x_in",))])
                        for grp, half, inside, cols_ in PIECES:
                            ins = dve.scalar_tensor_tensor(xT[:, arg, cols_], G[:, s, half, inside],
                                                           mod[:, v * KD + arg, grp:grp + 1], xT[:, arg, cols_],
                                                           ALU.mult, ALU.add)
                        ins.then_inc(done, 1)
                        wait_slot(dve, g)
                        add_square(arg)
                    elif kind == "ffu":
                        wait_group(dve, g)
                        wait_slot(dve, g - 1)
                        x = new_val(a_hi[:, arg, :], a_lo[:, arg, :])
                        dve.tensor_tensor(halves(x), slot_view(g), halves(g_act[:, arg % 2, :]), ALU.mult)\
                            .then_inc(done, 1)

        @block.tensor
        def _(pe):
            seen = dict(u=0, s=0)

            def fill(n, k, products):
                f = first_fill[n] + k
                if f >= 4:
                    wait_bank(pe, f - 4)
                for make in products:
                    ins = make(f % 4)
                ins.then_inc(fill_done, 1)

            def mm(out, lhsT, rhs, start=True, stop=True):
                return lambda b: pe.matmul(out(b), lhsT, rhs, start=start, stop=stop, skip_group_check=True)

            def tr(out, in_):
                return lambda b: pe.transpose(out(b), in_, ident[0:in_.shape[0], 0:in_.shape[0]])

            def each(cs):
                return [(i, c, h) for i, c in enumerate(cs) for h in range(2)]

            def sums_of(n, k, x):
                fill(n, k, [mm(lambda b: R[:, b, 0:SEQ], ones[:, :], x[:, 0:SEQ])])
                fill(n, k + 1, [mm(lambda b: R[:, b, 0:DEC], ones[:, :], x[:, SEQ:TOK])])

            def wait_lv(pair, lv):
                if lv == 0:
                    wait_bank(pe, last_bank[spot("g_x", pair, 0)])
                    pe.wait_ge(U0_ready, pair + 1)
                else:
                    wait_bank(pe, last_bank[spot("g_y", pair, lv)])

            pe.wait_ge(const_in, 48)
            for n, step in enumerate(plan):
                name, a = step[0], step[1:]
                if name == "job":
                    i = a[0]
                    job = jobs[i]
                    g = job.group
                    if job.first and g >= 2:
                        wait_slot(pe, g - 2)
                    if job.src == "c":
                        wait_weights(pe, i)
                        pe.wait_ge(c_sig, 1)
                        for k in range(KD):
                            ins = pe.matmul(G[:, g % 2, 0, job.col:job.col + 2], raw[:, i % 3, k, :], cT[:, :, k],
                                            start=(k == 0), stop=(k == KD - 1), skip_group_check=True)
                    else:
                        m = nth_split[i]
                        pe.wait_ge(w_lo_done, m + 1)
                        pe.wait_ge(lo_ready, vals_before[job.src] + job.k0 + job.nk)
                        hi, lo = src[job.src]
                        for half in range(2):
                            cols_ = slice(half * HALF, (half + 1) * HALF)
                            out = G[0:job.m, g % 2, half, 0:HALF]
                            for k in range(job.nk):
                                wh, wl = (w[:, m % 2, k, 0:job.m] for w in (w_hi, w_lo))
                                xh, xl = (x[:, job.k0 + k, cols_] for x in (hi, lo))
                                for p, (w, x) in enumerate(((wh, xh), (wh, xl), (wl, xh))):
                                    ins = pe.matmul(out, w, x, start=(job.first and k == 0 and p == 0),
                                                    stop=(job.last and k == job.nk - 1 and p == 2))
                    ins.then_inc(job_done, 1)
                elif name == "vectors":
                    pe.wait_ge(vec_in, 16 * 12)
                    fill(n, 0, [tr(lambda b: R[:, b, 0:NA], vecs[0:NA, 0, :])])
                    fill(n, 1, [tr(lambda b: R[:, b, 0:NB], vecs[0:NB, 1, :])])
                elif name == "x_in":
                    pe.wait_ge(x_in, 32 * (order[n] + 1))
                    for k in range(KD):
                        fill(n, k, [tr(lambda b, c=c: R[:, b, c * P:(c + 1) * P], xtok[:, c, k * P:(k + 1) * P])
                                    for c in range(N_CHUNK)])
                    fill(n, KD, [tr(lambda b, k=k: R[:, b, k * DEC:(k + 1) * DEC],
                                    xtok[0:DEC, N_CHUNK, k * P:(k + 1) * P]) for k in range(KD)])
                elif name == "sums":
                    pe.wait_ge(acc_ready, order[n] + 1)
                    sums_of(n, 0, acc[:, :])
                elif name == "onorm":
                    pe.wait_ge(sq_ready, head_norms[n] + 1)
                    sums_of(n, 0, sq[:, head_norms[n] % 2, :])
                elif name == "g_norm":
                    for k in range(4):
                        pe.wait_ge(sq_ready, head_norms[n] + k + 1)
                        sums_of(n, 2 * k, sq[:, (head_norms[n] + k) % 2, :])
                elif name == "g_rows":
                    pe.wait_ge(pg_ready, 1)
                    fill(n, 0, [tr(lambda b, c=c, j=j: R[0:length(c), b, c * 8 + 4 * j:c * 8 + 4 * j + 4],
                                   rows[:, (2, 3)[j], toks(c)]) for c in range(CHUNKS) for j in range(2)])
                elif name == "g_bcast":
                    pair = a[0]
                    for h in range(2):
                        fill(n, h, [mm(lambda b: R[:, b, 0:SEQ], sel[:, 2 * pair + h, :], rows[:, 0, 0:SEQ])])
                    fill(n, 2, [mm(lambda b, h=h: R[:, b, h * DEC:(h + 1) * DEC], sel[:, 2 * pair + h, :],
                                   rows[:, 0, SEQ:TOK]) for h in range(2)])
                elif name == "g_gram":
                    pair = a[0]
                    q0 = norms[spot("g_norm", pair)]
                    pe.wait_ge(rn_used, q0 + 4)
                    q, k_ = inp[:, pair, 0:2, :], inp[:, pair, 2:4, :]
                    for j, y in enumerate((k_, q)):
                        for k, cs in enumerate(FILLS):
                            fill(n, 3 * j + k, [mm(lambda b, i=i, h=h, cs=cs: fill_view(b, cs)[:, i, h, :],
                                                   k_[:, h, toks(c)], y[:, h, toks(c)]) for i, c, h in each(cs)])
                elif name in ("g_tok", "h_v"):
                    pair = a[0]
                    if name == "h_v":
                        wait_slot(pe, max(g for g, z in enumerate(groups) if z[0] == "hi" and z[1] == (pair, 1)))
                    for j, s in enumerate((4, 2) if name == "g_tok" else (4,)):
                        for k, cs in enumerate(FILLS):
                            fill(n, 3 * j + k, [tr(lambda b, i=i, h=h, cs=cs: fill_view(b, cs, False)[:, i, h, :],
                                                   inp[:, pair, s + h, toks(c)]) for i, c, h in each(cs)])
                    if name == "g_tok":
                        for h in range(2):
                            fill(n, 6 + h, [mm(lambda b: R[:, b, 0:SEQ], sel[:, 2 * pair + h, :], rows[:, 3, 0:SEQ])])
                        fill(n, 8, [mm(lambda b, h=h: R[:, b, h * DEC:(h + 1) * DEC], sel[:, 2 * pair + h, :],
                                       rows[:, 3, SEQ:TOK]) for h in range(2)])
                elif name == "g_x":
                    pair, lv = a
                    pe.wait_ge(Nl_ready, order[n] + 1)
                    if lv:
                        wait_lv(pair, lv - 1)
                    for k, cs in enumerate(FILLS if lv < 5 else FILLS[:2]):
                        fill(n, k, [mm(lambda b, i=i, h=h, cs=cs: fill_view(b, cs)[:, i, h, :],
                                       Nl[0:length(c), c, h, 0:length(c)],
                                       Tm[0:length(c), c, h, 0:length(c)] if lv else
                                       ident[0:length(c), 0:length(c)]) for i, c, h in each(cs)])
                elif name == "g_y":
                    pair, lv = a
                    wait_bank(pe, last_bank[spot("g_x", pair, lv)])
                    k = 0
                    for l_, r_ in (((Um, X), (X, Um)) if lv < LEVELS - 1 else ((X, Um),)):
                        for cs in (FILLS if lv < 5 else FILLS[:2]):
                            fill(n, k, [mm(lambda b, i=i, h=h, cs=cs: fill_view(b, cs)[:, i, h, :],
                                           l_[0:length(c), c, h, 0:length(c)], r_[0:length(c), c, h, 0:length(c)])
                                        for i, c, h in each(cs)])
                            k += 1
                elif name == "g_w":
                    pair = a[0]
                    wait_lv(pair, LEVELS - 1)
                    wait_bank(pe, first_fill[spot("g_tok", pair)] + 5)
                    for k, cs in enumerate(FILLS):
                        fill(n, k, [mm(lambda b, i=i, h=h, cs=cs: feat_view(b, cs)[:, i, h, :],
                                       kPG[0:length(c), c, h, :], Um[0:length(c), c, h, 0:length(c)])
                                    for i, c, h in each(cs)])
                elif name == "g_u":
                    pair, c = a
                    L = length(c)
                    u = unit(name, pair)
                    wait_bank(pe, last_bank[spot("g_w", pair)])
                    wait_bank(pe, last_bank[spot("g_tok", pair)])
                    if c == N_CHUNK:
                        pe.wait_ge(state_in, 16 * (u + 1))
                    if seen["s"]:
                        wait_bank(pe, last_state(n))
                    s_at = 2 if c == N_CHUNK else c % 2
                    make = []
                    for h in range(2):
                        out = (lambda b, h=h: R[0:L, b, h * P:(h + 1) * P])
                        make.append(mm(out, Um[0:L, c, h, 0:L], v_tok[0:L, pair, c, h, :], True, c == 0))
                        if c:
                            make.append(mm(out, Wn[:, c, h, 0:L], S[:, s_at, h, :], False, True))
                    fill(n, 0, make)
                elif name in ("g_o", "h_o"):
                    pair, c = a
                    L = length(c)
                    u = unit(name, pair)
                    s_at = 2 if c == N_CHUNK else c % 2
                    if name == "g_o":
                        wait_bank(pe, first_fill[n] - 1)
                        kt, vt, sc = kD, (lambda h: u_tok[0:L, h, :]), PT
                    else:
                        wait_bank(pe, last_bank[spot("h_k", pair)])
                        if c == N_CHUNK:
                            pe.wait_ge(state_in, 16 * (u + 1))
                        wait_bank(pe, last_state(n))
                        kt, vt, sc = kD, (lambda h: v_tok[0:L, pair, c, h, :]), PT
                    seen["s"] += 1
                    make = []
                    for h in range(2):
                        out = (lambda b, h=h: R[:, b, h * L:(h + 1) * L])
                        make.append(mm(out, vt(h), sc[0:L, c, h, 0:L], True, c == 0))
                        if c:
                            make.append(mm(out, S[:, s_at, h, :], inp[:, pair, h, toks(c)], False, True))
                    fill(n, 0, make)
                    fill(n, 1, [mm(lambda b, h=h: R[:, b, h * P:(h + 1) * P], kt[0:L, c, h, :], vt(h))
                                for h in range(2)])
                elif name in ("h_diag", "h_level"):
                    pair = a[0]
                    if name == "h_diag":
                        wait_slot(pe, max(g for g, z in enumerate(groups) if z[0] == "hf" and z[1] == (pair, 1)))
                        todo = FILLS
                    else:
                        pe.wait_ge(hg_ready, order[n] + pair + 1)
                        todo = FILLS if a[1] < 5 else FILLS[:2]
                    for k, cs in enumerate(todo):
                        fill(n, k, [mm(lambda b, i=i, h=h, cs=cs: fill_view(b, cs)[:, i, h, :],
                                       inp[:, pair, 2 + h, toks(c)], inp[:, pair, h, toks(c)]) for i, c, h in each(cs)])
                elif name == "h_k":
                    pair = a[0]
                    pe.wait_ge(hg_ready, (LEVELS + 1) * (pair + 1))
                    for k, cs in enumerate(FILLS):
                        fill(n, k, [tr(lambda b, i=i, h=h, cs=cs: fill_view(b, cs, False)[:, i, h, :],
                                       inp[:, pair, 2 + h, toks(c)]) for i, c, h in each(cs)])
                elif name == "conv_out":
                    pe.wait_ge(ext_ready, 12)
                    fill(n, 0, [tr(lambda b: R[0:72, b, 0:P], conv_keep[:, :, :, :].rearrange("p g j n -> p (g j n)"))])
                elif name == "y_out":
                    pe.wait_ge(yT_ready, KD)
                    for c in range(CHUNKS):
                        L = length(c)
                        for j in range(2):
                            fill(n, 2 * c + j, [tr(lambda b, k=k: R[0:L, b, k * P:(k + 1) * P],
                                                   xT[:, 4 * j + k, toks(c)]) for k in range(4)])


_INS = ["x_prompt", "x_sample", "state_hgrn", "state_gdn", "state_conv", "c_prompt", "c_sample", "w_ada",
        "b_ada", "norm_mix", "w_in", "hg_lb", "hg_norm", "conv_w", "gdn_a_log", "gdn_dt_bias", "gdn_norm",
        "w_proj_a", "w_proj_b", "w_out", "norm_ffn", "w_up", "w_down", "final_norm"]
_OUTS = [(1, SEQ, D), (1, DEC, D), (1, 1, NH, P, P), (1, 1, NH, P, P), (1, 1, CONV_W - 1, 12 * P),
         (1, 1, NH, P, P), (1, 1, NH, P, P), (1, 1, CONV_W - 1, 12 * P)]


def constants():
    s, tt = np.arange(P)[:, None], np.arange(P)[None, :]
    levels = [((s >> lv) % 2 == 0) & ((tt >> lv) % 2 == 1) & (s >> (lv + 1) == tt >> (lv + 1))
              for lv in range(LEVELS)] + [s == tt]
    select = np.zeros((NH, NH, P), np.float32)
    for h in range(NH):
        select[h, h] = 1
    return {"level_masks": np.stack(levels, 1).astype(np.float32), "all_ones": np.ones((P, P), np.float32),
            "head_select": select}


def kernel(**inputs):
    import concourse.bacc as _bacc
    from concourse.bass_utils import run_bass_kernel_spmd as _run

    nc = _bacc.Bacc("TRN2", target_bir_lowering=False, num_devices=1)
    arrays, t = {}, {}
    for name, value in [*((n, inputs[n]) for n in _INS), *constants().items()]:
        a = np.ascontiguousarray(value)
        arrays[f"in_{name}"] = a
        t[name] = nc.dram_tensor(f"in_{name}", a.shape, mybir.dt.from_np(a.dtype), kind="ExternalInput").ap()
    for name, short in (("w_ada", "w_ada"), ("w_in", "w_in"), ("w_proj_a", "w_pa"), ("w_proj_b", "w_pb"),
                        ("w_out", "w_out"), ("w_up", "w_up"), ("w_down", "w_down")):
        t[short] = t[name][0]
    outs = [nc.dram_tensor(f"out_{i}", shape, F32, kind="ExternalOutput").ap() for i, shape in enumerate(_OUTS)]
    build(nc, t, outs)
    r = _run(nc, [arrays], core_ids=[0])
    return tuple(r.results[0][f"out_{i}"] for i in range(len(_OUTS)))
```

```python
from contextlib import ExitStack

import numpy as np

import concourse.bass as bass
from concourse import mybir

F32 = mybir.dt.float32
F32R = mybir.dt.float32r
U32 = mybir.dt.uint32
ALU = mybir.AluOpType
ACT = mybir.ActivationFunctionType

P = 128
D = 1024
KD = D // P
SEQ, DEC = 512, 32
TOK = SEQ + DEC
HALF = TOK // 2
NH = 4
CONV_W = 4
D_FF = 2816
KF = D_FF // P
EPS = 1e-6
RAW = 4
LEVELS = 7
N_CHUNK = SEQ // P
CHUNKS = N_CHUNK + 1
FILLS = [(0, 1), (2, 3), (4,)]
QSCALE = float(P) ** -0.5
COL = dict(hq=0, hf=512, hi=1024, hog=1536, gq=2048, gk=2560, gv=3072, gagb=3584, gz=3592,
           gate_a=4104, gate_b=5128)
EXT = CONV_W - 1 + SEQ + CONV_W - 1 + DEC
CO = EXT - (CONV_W - 1)
SMP = SEQ + CONV_W - 1
VA = dict(b_ada=0, conv_w=48)
VB = dict(norm_mix=0, norm_ffn=8, final=16, hg=24, gdn=25, c=26, conv_state=42)
NA, NB = 96, 78


def length(c):
    return P if c < N_CHUNK else DEC


class Job:

    def __init__(self, w, nk, src, k0, group, first, last, m=P, pieces=None):
        self.w, self.nk, self.src, self.k0, self.group = w, nk, src, k0, group
        self.first, self.last, self.m, self.pieces = first, last, m, pieces


def make_plan(t):
    jobs, groups, plan = [], [], []

    def tile(w, c0, m=P):
        return w[:, c0:c0 + m].rearrange("(k p) m -> p k m", p=P)

    def add(kind, arg, parts):
        g = len(groups)
        for n, part in enumerate(parts):
            plan.append(("job", len(jobs)))
            if part["src"] != "c":
                plan.append(("half", len(jobs)))
            jobs.append(Job(group=g, first=(n == 0), last=(n == len(parts) - 1), **part))
        groups.append((kind, arg, len(jobs) - 1))
        plan.append(("evac", g))

    def ada(v, n):
        add("ada", (v, n), [dict(w=tile(t["w_ada"], v * D + n * P), nk=KD, src="c", k0=0)])

    def proj(kind, arg, c0):
        add(kind, arg, [dict(w=tile(t["w_in"], c0), nk=KD, src="h", k0=0)])

    def do(name, *arg):
        plan.append((name, *arg))

    def gdn_inputs(pair):
        return [lambda name=name, slot=slot, h=h:
                proj("conv", (name, pair, h, slot + h), COL[name] + (2 * pair + h) * P)
                for name, slot in (("gk", 2), ("gq", 0), ("gv", 4)) for h in range(2)]

    def hg_inputs(pair):
        def one(name, h):
            proj(name, (pair, h), COL[name] + (2 * pair + h) * P)
            if name == "hi" and h == 1:
                do("h_v", pair)
        return [lambda name=name, h=h: one(name, h) for name in ("hi", "hq", "hf") for h in range(2)]

    later_ada = [(v, n) for v in range(2, 6) for n in range(KD)]

    def ada_part(count):
        part = [later_ada.pop(0) for _ in range(count)]
        return [lambda v=v, n=n: ada(v, n) for v, n in part]

    def braid(a, b):
        out, j = [], 0
        for i, x in enumerate(a):
            out.append(x)
            while j < len(b) and (j + 1) * len(a) <= (i + 1) * len(b):
                out.append(b[j])
                j += 1
        return out + b[j:]

    do("vectors")
    do("x_in")
    do("ada_q", 0)
    do("ada_q", 1)
    do("sums")
    do("x_norm")
    do("ada_q", 2)
    do("ada_q", 3)
    do("ada_T")
    do("h1")
    add("gagb", 0, [dict(w=None, pieces=[(t["w_in"][:, 3584:3588].rearrange("(k p) m -> p k m", p=P), 0),
                                         (t["w_in"][:, 3588:3592].rearrange("(k p) m -> p k m", p=P), 32)],
                         nk=KD, src="h", k0=0, m=36)])

    def gdn_steps(pair):
        s = [("g_sq", pair)] + [("g_norm", pair, k) for k in range(4)]
        s += [("g_bcast", pair), ("g_gram", pair), ("g_tok", pair)]
        for lv in range(LEVELS):
            s.append(("g_x", pair, lv))
            if lv:
                s.append(("g_y", pair, lv))
        s.append(("g_w", pair))
        for c in (0, 4, 1, 2, 3):
            s += [("g_u", pair, c), ("g_o", pair, c)]
        s.append(("g_end", pair))
        return s

    def hg_steps(pair):
        s = ([("conv_out",)] if pair == 0 else []) + [("h_diag", pair)]
        s += [("h_level", pair, lv) for lv in range(LEVELS)]
        s.append(("h_k", pair))
        s += [("h_o", pair, c) for c in (0, 4, 1, 2, 3)]
        s.append(("h_end", pair))
        return s

    def mixed(steps, work):
        mark = len(plan)
        for w in work:
            w()
        parts = []
        for s in plan[mark:]:
            if s[0] in ("job", "half"):
                parts.append([])
            parts[-1].append(s)
        del plan[mark:]
        done = 0
        for n, s in enumerate(steps):
            while done * len(steps) <= n * len(parts) and done < len(parts):
                plan.extend(parts[done])
                done += 1
            plan.append(s)
        for part in parts[done:]:
            plan.extend(part)

    for w, after in zip(gdn_inputs(0), ("g_sp", "g_a", "g_scan", "g_rows", None, None)):
        w()
        if after:
            do(after)
    og = [lambda n=n: proj("og", n, COL["hog" if n < NH else "gz"] + n % NH * P) for n in range(2 * NH)]
    mixed(gdn_steps(0), braid(gdn_inputs(1), ada_part(8)))
    mixed(gdn_steps(1), braid(hg_inputs(0), ada_part(8)))
    def norm_steps(heads):
        return [(name, n) for n in heads for name in ("o_sq", "onorm")]

    mixed(braid(hg_steps(0), norm_steps(range(NH, 2 * NH))), braid(hg_inputs(1), ada_part(6)))
    mixed(braid(hg_steps(1), norm_steps(range(2))), braid(og[:6], ada_part(10)))
    mixed([("o_sq", 2), ("o_sq", 3), ("onorm", 2), ("onorm", 3)] + [("ogate", n) for n in range(NH)], og[6:])
    for m in range(KD):
        proj("gate", ("a", m), COL["gate_a"] + m * P)
        if m == 0:
            do("ogate", NH)
            do("ogate", NH + 1)
        proj("gate", ("b", m), COL["gate_b"] + m * P)
        if m == 0:
            do("ogate", NH + 2)
            do("ogate", NH + 3)
        add("pa", m, [dict(w=tile(t["w_pa"], m * P), nk=NH, src="o", k0=0)])
        add("pb", m, [dict(w=tile(t["w_pb"], m * P), nk=NH, src="o", k0=NH)])
        if m == 1:
            do("x_load")
        if m == 4:
            do("x_in")
    for m in range(KD):
        add("out", m, [dict(w=tile(t["w_out"], m * P), nk=KD, src="y", k0=0)])
    do("sums")
    do("h2")
    for m in range(KF):
        add("ffg", m, [dict(w=tile(t["w_up"], m * P), nk=KD, src="h2", k0=0)])
        add("ffu", m, [dict(w=tile(t["w_up"], D_FF + m * P), nk=KD, src="h2", k0=0)])
    for m in range(KD):
        parts = []
        for k0 in range(0, KF, KD):
            nk = min(KD, KF - k0)
            parts.append(dict(w=t["w_down"][k0 * P:(k0 + nk) * P, m * P:(m + 1) * P]
                              .rearrange("(k p) m -> p k m", p=P), nk=nk, src="a", k0=k0))
        add("down", m, parts)
    do("sums")
    do("y_out")
    return jobs, groups, plan


def bank_users(step):
    name, a = step[0], step[1:]
    n = len(FILLS)
    short = n if name not in ("g_x", "g_y", "h_level") or a[1] < 5 else n - 1
    return {
        "vectors": ["dve"] * 2, "x_in": ["act"] * (KD + 1), "sums": ["act"] * 2, "onorm": ["act"] * 2,
        "ada_q": ["act"], "ada_T": ["dve"], "g_rows": ["dve"], "g_norm": ["act"] * 2, "g_bcast": ["act"] * n, "g_gram": ["dve"] * (2 * n),
        "g_tok": ["act"] * n + ["dve"] * (2 * n),
        "g_x": ["dve" if name == "g_x" and a[1] == 0 else "act"] * short,
        "g_y": ["dve"] * (short if name == "g_y" and a[1] == LEVELS - 1 else 2 * short),
        "g_w": ["act"] * n, "g_u": ["dve"], "g_o": ["act", "dve"],
        "conv_out": ["act"], "h_v": ["act"] * n, "h_diag": ["dve"] * n, "h_level": ["dve"] * short,
        "h_k": ["act"] * n, "h_o": ["act", "dve"], "y_out": ["act"] * (2 * CHUNKS),
    }.get(name, [])


GROUP_USER = dict(ada="dve", gagb="dve", conv="act", hi="act", hq="act", hf="act", og="act",
                  gate="act", pa="dve", pb="dve", out="dve", ffg="act", ffu="dve", down="dve")


def build(nc, t, outs):
    jobs, groups, plan = make_plan(t)
    y_p, y_s, hg_p, gdn_p, conv_p, hg_s, gdn_s, conv_s = outs

    first_fill, freed, slot_freed = [], [], []
    count = dict(act=0, dve=0)
    for step in plan:
        first_fill.append(len(freed))
        for user in bank_users(step):
            count[user] += 1
            freed.append((user, count[user]))
    count = dict(act=0, dve=0)
    for kind, _, _ in groups:
        count[GROUP_USER[kind]] += 1
        slot_freed.append((GROUP_USER[kind], count[GROUP_USER[kind]]))
    split = [i for i, j in enumerate(jobs) if j.src != "c"]
    nth_split = {i: n for n, i in enumerate(split)}
    vals_before = dict(h=0, o=KD, y=2 * KD, h2=3 * KD, a=4 * KD)
    def nth(at):
        return sum(s[0] == plan[at][0] for s in plan[:at])

    order = [nth(n) for n in range(len(plan))]
    units = [s for s in plan if s[0] in ("g_end", "h_end")]

    ctx = ExitStack()
    with ctx:
        def sb(name, shape, dt=F32):
            return ctx.enter_context(nc.sbuf_tensor(name, shape, dt))

        def sem(name):
            return ctx.enter_context(nc.semaphore(name))

        masks = sb("masks", [P, LEVELS + 1, P])
        ones = sb("ones", [P, P])
        sel = sb("sel", [NH, NH, P])
        ident = masks[:, LEVELS, :]
        vecs = sb("vecs", [P, 2, P])
        vT = sb("vT", [P, NA + NB])
        cT = sb("cT", [P, 2, KD])
        mod = sb("mod", [P, 6 * KD, 2])
        gain = sb("gain", [P, 2, KD])
        eps = sb("eps", [P, 1])
        warm = sb("warm", [P, 1])
        vec4 = sb("vec4", [NH, 4])
        raw = sb("raw", [P, RAW, KD, P])
        w_hi = sb("w_hi", [P, 2, KD, P], F32R)
        w_lo = sb("w_lo", [P, 2, KD, P], F32R)
        h_hi = sb("h_hi", [P, KD, TOK], F32R)
        h_lo = sb("h_lo", [P, KD, TOK], F32R)
        rn = sb("rn", [P, 2, TOK])
        sq = sb("sq", [P, 2, TOK])
        acc = sb("acc", [P, TOK])
        val = sb("val", [P, 2, TOK])
        base = (nc.sbuf_base + 31) // 32 * 32

        room = 229344 - base
        where = dict(rec=base, mix=base, ffn=base)

        def at(phase, name, shape, dt=F32, off=None):
            if off is None:
                off = where[phase]
                where[phase] = off + (int(np.prod(shape[1:])) * 4 + 31) // 32 * 32
                assert where[phase] <= base + room, (phase, name, where[phase] - base, room)
            return nc.alloc_sbuf_tensor_at(name, shape, dt, offset=off)

        row, tile = TOK * 4, CHUNKS * 2 * P * 4
        xT = at("rec", "xT", [P, KD, TOK])
        o = at("rec", "o", [P, 2 * NH, TOK])
        rows = at("rec", "rows", [NH, 4, TOK], off=base + KD * row)
        xtok = at("rec", "xtok", [P, CHUNKS, D], off=base + 45 * row)
        wada01 = at("rec", "wada01", [P, KD, 2 * D], off=base + KD * row)
        ada_rows = at("rec", "ada_rows", [2, 2 * D], off=base + 40 * row)
        inp = at("rec", "inp", [P, 2, 6, TOK])
        ext = at("rec", "ext", [P, EXT])
        cy = at("rec", "cy", [P, CO])
        conv_keep = at("rec", "conv_keep", [P, 2, CONV_W - 1, 12])
        conv_rows = at("rec", "conv_rows", [2 * 12 * (CONV_W - 1), P])
        cols = at("rec", "cols", [P, CHUNKS, 2, NH])
        v_tok = at("rec", "v_tok", [P, 2, CHUNKS, 2, P])
        S = at("rec", "S", [P, 3, 2, P])
        relT = at("rec", "relT", [P, CHUNKS, 2, P])
        N = at("rec", "N", [P, CHUNKS, 2, P], off=base + 0 * tile)
        PT = at("rec", "PT", [P, CHUNKS, 2, P], off=base + 1 * tile)
        Tm = at("rec", "Tm", [P, CHUNKS, 2, P], off=base + 2 * tile)
        Um = at("rec", "Um", [P, CHUNKS, 2, P])
        X = at("rec", "X", [P, CHUNKS, 2, P])
        Wn = X
        Nl = at("rec", "Nl", [P, CHUNKS, 2, P])
        abc = at("rec", "abc", [P, 2, TOK], off=where["rec"] - CHUNKS * 2 * P * 4)
        kPG = at("rec", "kPG", [P, CHUNKS, 2, P])
        o_gate = at("rec", "o_gate", [P, 2 * NH, TOK], off=where["rec"] - 5 * tile)
        kD = at("rec", "kD", [P, CHUNKS, 2, P])
        u_tok = at("rec", "u_tok", [P, 2, P])
        elast = at("rec", "elast", [P, CHUNKS, 2])

        where["mix"] += 2 * KD * row
        o_hi = at("mix", "o_hi", [P, 2 * NH, TOK], F32R)
        o_lo = at("mix", "o_lo", [P, 2 * NH, TOK], F32R)
        gate = at("mix", "gate", [P, 2, TOK])
        ya = at("mix", "ya", [P, 2, TOK])
        assert where["mix"] == base + 36 * row
        y_hi = at("mix", "y_hi", [P, KD, TOK], F32R)
        y_lo = at("mix", "y_lo", [P, KD, TOK], F32R, off=base + KD * row)
        where["ffn"] += (KD + 2) * row
        a_hi = at("ffn", "a_hi", [P, KF, TOK], F32R)
        a_lo = at("ffn", "a_lo", [P, KF, TOK], F32R)
        g_act = at("ffn", "g_act", [P, 2, TOK], off=base + KD * row)
        ytok = at("ffn", "ytok", [P, CHUNKS, D], off=base + 16 * row)
        src = dict(h=(h_hi, h_lo), o=(o_hi, o_lo), y=(y_hi, y_lo), h2=(h_hi, h_lo), a=(a_hi, a_lo))

        G = ctx.enter_context(nc.psum_tensor("G", [P, 2, 2, 512], F32))
        R = ctx.enter_context(nc.psum_tensor("R", [P, 4, 512], F32))

        const_in = sem("const_in")
        vec_in = sem("vec_in")
        x_in = sem("x_in")
        ada_in = [sem(f"ada_in{k}") for k in range(4)]
        w_in = [sem(f"w_in{n}") for n in range(RAW)]
        w_hi_done = sem("w_hi_done")
        w_lo_done = sem("w_lo_done")
        job_done = sem("job_done")
        slot_user = dict(act=sem("slot_read_act"), dve=sem("slot_read_dve"))
        fill_done = sem("fill_done")
        bank_user = dict(act=sem("bank_read_act"), dve=sem("bank_read_dve"))
        eps_set = sem("eps_set")
        c_sig = sem("c_sig")
        acc_ready = sem("acc_ready")
        sq_ready = sem("sq_ready")
        rn_ready = sem("rn_ready")
        rn_used = sem("rn_used")
        val_ready = sem("val_ready")
        hi_ready = sem("hi_ready")
        lo_ready = sem("lo_ready")
        dve_step = sem("dve_step")
        act_step = sem("act_step")
        ext_ready = sem("ext_ready")
        cy_ready = sem("cy_ready")
        conv_ready = sem("conv_ready")
        hist_zero = sem("hist_zero")
        pad_zero = sem("pad_zero")
        x_rows = sem("x_rows")
        sp_log = sem("sp_log")
        sp_ready = sem("sp_ready")
        a_ready = sem("a_ready")
        pg_ready = sem("pg_ready")
        Nl_ready = sem("Nl_ready")
        U0_ready = sem("U0_ready")
        at_zero = sem("at_zero")
        hg_ready = sem("hg_ready")
        state_in = sem("state_in")
        state_out = sem("state_out")
        yT_ready = sem("yT_ready")
        y_out = sem("y_out")
        conv_sent = sem("conv_sent")

        def toks(c):
            return slice(c * P, c * P + length(c))

        def fill_view(bank, cs, square=True):
            L = length(cs[0])
            w = L if square else P
            return R[0:L if square is not None else P, bank, 0:len(cs) * 2 * w].rearrange(
                "p (c h t) -> p c h t", c=len(cs), h=2)

        def feat_view(bank, cs):
            L = length(cs[0])
            return R[:, bank, 0:len(cs) * 2 * L].rearrange("p (c h t) -> p c h t", c=len(cs), h=2)

        def heads_view(slots, cs):
            L = length(cs[0])
            return slots[:, :, cs[0] * P:cs[0] * P + len(cs) * L].rearrange("p h (c t) -> p c h t", t=L)

        def bc(ap, n):
            return ap.unsqueeze(len(ap.shape)).broadcast_to([*ap.shape, n])

        def mid(ap, n):
            return ap.unsqueeze(1).broadcast_to([ap.shape[0], n, ap.shape[1]])

        def slot_view(g):
            return G[:, g % 2, :, 0:HALF]

        def halves(ap):
            return ap.rearrange("p (n t) -> p n t", n=2)

        def wait_bank(eng, n):
            who, k = freed[n]
            eng.wait_ge(bank_user[who], k)

        def wait_slot(eng, g, walk=None):
            who, k = slot_freed[g]
            eng.wait_ge(slot_user[who], walk.plus(k, 2) if walk else k)

        def wait_group(eng, g, walk=None):
            done = groups[g][2] + 1
            eng.wait_ge(job_done, walk.plus(done, 4) if walk else done)

        PIECES = [(0, 0, slice(0, HALF), slice(0, HALF)),
                  (0, 1, slice(0, SEQ - HALF), slice(HALF, SEQ)),
                  (1, 1, slice(SEQ - HALF, HALF), slice(SEQ, TOK))]
        GROUPS = [slice(0, SEQ), slice(SEQ, TOK)]
        norms = {}
        for n, s in enumerate(plan):
            norms[n] = sum(dict(sums=1, onorm=1, g_norm=1).get(x[0], 0) for x in plan[:n])
        head_norms = {n: sum(dict(onorm=1, g_norm=1).get(x[0], 0) for x in plan[:n]) for n in range(len(plan))}
        last_bank = {n: first_fill[n] + len(bank_users(s)) - 1 for n, s in enumerate(plan)}

        def spot(*step):
            return plan.index(step)

        up = [spot("job", next(i for i, j in enumerate(jobs) if groups[j.group][:2] == ("ffg", m)))
              for m in (2, 4, KF - 2)]
        TURNS = KF // 2 - 2

        class Walk:

            def __init__(self, eng):
                self.eng, self.turn, self.passed = eng, None, 0

            def __iter__(self):
                yield from enumerate(plan[:up[0]])
                with self.eng.Fori(0, TURNS) as turn:
                    self.turn = turn
                    yield from ((n, plan[n]) for n in range(up[0], up[1]))
                self.turn, self.passed = None, TURNS - 1
                yield from ((n, plan[n]) for n in range(up[2], len(plan)))

            def plus(self, value, each):
                return value if self.turn is None else self.turn * each + value

        def joined(x, cs):
            L = length(cs[0])
            return x[0:L, cs[0]:cs[-1] + 1, :, 0:L].rearrange("p c h t -> p (c h) t")

        def out_view(h0, c):
            return o[:, h0:h0 + 2, toks(c)]

        def copy_scores(dve, read, bank, n, lv):
            for k in range(len(bank_users(plan[n]))):
                cs = FILLS[k]
                b = bank(n, k)
                L = length(cs[0])
                m = 2 * len(cs)
                read(dve.copy_predicated(joined(PT, cs), mid(masks[0:L, lv, 0:L].bitcast(U32), m),
                                         R[0:L, b, 0:m * L].rearrange("p (m t) -> p m t", m=m)))

        groups_at = {(kind, arg): g for g, (kind, arg, _) in enumerate(groups)}

        def last_state(n):
            return last_bank[max(i for i in range(n) if plan[i][0] in ("g_o", "h_o"))]

        def unit(name, pair):
            return pair if name[0] == "g" else 2 + pair

        block = ctx.enter_context(nc.Block())

        @block.sync
        def _(sp):
            walk = Walk(sp)
            sp.dma_start(masks[:, :, :], t["level_masks"]).then_inc(const_in, 16)
            sp.dma_start(vecs[0:48, 0, :], t["b_ada"].rearrange("l (n p) -> (l n) p", p=P)).then_inc(vec_in, 16)
            sp.dma_start(vecs[48:96, 0, :], t["conv_w"].rearrange("l j (n p) -> (l j n) p", p=P)).then_inc(vec_in, 16)
            for name, key in (("norm_mix", "norm_mix"), ("norm_ffn", "norm_ffn")):
                r = VB[key]
                sp.dma_start(vecs[r:r + 8, 1, :], t[name].rearrange("l (n p) -> (l n) p", p=P)).then_inc(vec_in, 16)
            sp.dma_start(vecs[16:24, 1, :], t["final_norm"].rearrange("(n p) -> n p", p=P)).then_inc(vec_in, 16)
            sp.dma_start(vecs[24:25, 1, :], t["hg_norm"]).then_inc(vec_in, 16)
            sp.dma_start(vecs[25:26, 1, :], t["gdn_norm"]).then_inc(vec_in, 16)
            sp.dma_start(vecs[26:34, 1, :], t["c_prompt"].rearrange("l (n p) -> (l n) p", p=P)).then_inc(vec_in, 16)
            sp.dma_start(vecs[34:42, 1, :], t["c_sample"].rearrange("l (n p) -> (l n) p", p=P)).then_inc(vec_in, 16)
            sp.dma_start(vecs[42:78, 1, :], t["state_conv"].rearrange("l b j (n p) -> (l b j n) p", p=P)).then_inc(vec_in, 16)
            sp.dma_start(vec4[:, 0:1], t["gdn_dt_bias"].rearrange("l h -> h l")).then_inc(vec_in, 16)
            sp.dma_start(vec4[:, 1:2], t["gdn_a_log"].rearrange("l h -> h l")).then_inc(vec_in, 16)
            sp.dma_start(ones[:, :], t["all_ones"]).then_inc(const_in, 16)
            sp.dma_start(sel[:, :, :], t["head_select"]).then_inc(const_in, 16)
            for k in range(4):
                sp.dma_start(wada01[:, :, 512 * k:512 * (k + 1)],
                             t["w_ada"][:, 512 * k:512 * (k + 1)].rearrange("(k p) m -> p k m", p=P)).then_inc(ada_in[k], 16)
            for n, step in walk:
                if step[0] == "x_load":
                    wait_bank(sp, last_bank[spot("h_o", 1, 3)])
                    sp.wait_ge(state_out, 32 * len(units))
                    sp.dma_start(xtok[:, 0:N_CHUNK, :], t["x_prompt"].rearrange("b (c p) d -> p (b c) d", p=P)).then_inc(x_in, 16)
                    sp.dma_start(xtok[0:DEC, N_CHUNK, :], t["x_sample"].rearrange("b p d -> (b p) d")).then_inc(x_in, 16)
                if step[0] == "job":
                    i = step[1]
                    if i >= RAW:
                        if jobs[i - RAW].src == "c":
                            sp.wait_ge(job_done, i - RAW + 1)
                        else:
                            sp.wait_ge(w_hi_done, walk.plus(nth_split[i - RAW] + 1, 4))
                            sp.wait_ge(w_lo_done, walk.plus(nth_split[i - RAW] + 1, 4))
                    job = jobs[i]
                    if job.pieces:
                        sp.wait_ge(pad_zero, 1)
                        for piece, c0 in job.pieces:
                            sp.dma_start(raw[:, i % RAW, 0:job.nk, c0:c0 + NH], piece).then_inc(w_in[i % RAW], 16)
                    elif walk.turn is not None:
                        kind, m, _ = groups[job.group]
                        c0 = walk.plus((D_FF if kind == "ffu" else 0) + m * P, 2 * P)
                        sp.dma_start(raw[:, i % RAW, :, :], t["w_up"].rearrange("(k p) m -> p k m", p=P)
                                     [:, :, bass.ds(c0, P)]).then_inc(w_in[i % RAW], 16)
                    else:
                        sp.dma_start(raw[:, i % RAW, 0:job.nk, 0:job.m], job.w).then_inc(w_in[i % RAW], 16)
            for j in range(2):
                for c in range(CHUNKS):
                    wait_bank(sp, first_fill[spot("y_out")] + CHUNKS * j + c)
                    dst = y_p[0, toks(c), :] if c < N_CHUNK else y_s[0]
                    sp.dma_start(dst[:, j * 512:(j + 1) * 512], ytok[0:length(c), c, j * 512:(j + 1) * 512])\
                        .then_inc(y_out, 16)
            sp.wait_ge(y_out, 16 * 2 * CHUNKS)
            sp.wait_ge(conv_sent, 32)
            sp.wait_ge(state_out, 16 * 2 * len(units))

        landed = {}
        total = [0] * RAW
        for i, job in enumerate(jobs):
            total[i % RAW] += 16 * (len(job.pieces) if job.pieces else 1)
            landed[i] = total[i % RAW]

        def wait_weights(eng, i, walk):
            eng.wait_ge(w_in[i % RAW], walk.plus(landed[i], 16))

        @block.gpsimd
        def _(pool):
            walk = Walk(pool)
            pool.memset(raw[:, 0, :, 0:36], 0.0).then_inc(pad_zero, 1)

            def load_state(u):
                name = "state_gdn" if u < 2 else "state_hgrn"
                pair = u % 2
                pool.dma_start(S[:, 2, :, :], t[name][0, 0, 2 * pair:2 * pair + 2].rearrange("h d v -> d h v"))\
                    .then_inc(state_in, 16)

            for n, step in walk:
                name = step[0]
                if name == "g_sq" and step[1] == 0:
                    pool.wait_ge(fill_done, last_bank[spot("ada_T")] + 1)
                    load_state(0)
                if name == "g_x":
                    pair, lv = step[1:]
                    wait_bank(pool, first_fill[spot("g_gram", pair)] + 2)
                    if lv:
                        pool.wait_ge(fill_done, last_bank[spot("g_x", pair, lv - 1)] + 1)
                    if lv == 1:
                        pool.wait_ge(U0_ready, pair + 1)
                    if lv < 5:
                        pool.tensor_tensor(Nl[0:DEC, N_CHUNK, :, 0:DEC], N[0:DEC, N_CHUNK, :, 0:DEC],
                                           mid(masks[0:DEC, lv, 0:DEC], 2), ALU.mult)
                    pool.tensor_tensor(Nl[:, 0:N_CHUNK, :, :].rearrange("p c h t -> p (c h) t"),
                                       N[:, 0:N_CHUNK, :, :].rearrange("p c h t -> p (c h) t"),
                                       mid(masks[:, lv, :], 2 * N_CHUNK), ALU.mult).then_inc(Nl_ready, 1)
                    if lv == 0:
                        pool.wait_ge(Nl_ready, order[n] + 1)
                        pool.tensor_tensor(Um[0:DEC, N_CHUNK, :, 0:DEC], mid(ident[0:DEC, 0:DEC], 2),
                                           Nl[0:DEC, N_CHUNK, :, 0:DEC], ALU.subtract)
                        pool.tensor_tensor(Um[:, 0:N_CHUNK, :, :].rearrange("p c h t -> p (c h) t"),
                                           mid(ident, 2 * N_CHUNK),
                                           Nl[:, 0:N_CHUNK, :, :].rearrange("p c h t -> p (c h) t"),
                                           ALU.subtract).then_inc(U0_ready, 1)
                if name == "h_diag":
                    prev = units[unit(name, step[1]) - 1]
                    pool.wait_ge(fill_done, last_bank[plan.index(prev) - 1] + 1)
                    pool.memset(PT[:, :, :, :], 0.0).then_inc(at_zero, 1)
                if name == "conv_out":
                    wait_bank(pool, first_fill[n])
                    m = 12 * (CONV_W - 1)
                    for g, out in enumerate((conv_p, conv_s)):
                        pool.dma_start(out.rearrange("l b j (n p) -> (l b j n) p", p=P),
                                       conv_rows[g * m:(g + 1) * m, :]).then_inc(conv_sent, 16)
                if name in ("g_end", "h_end"):
                    u = unit(name, step[1])
                    pair = step[1]
                    wait_bank(pool, last_bank[n - 1])
                    for part, out in ((0, gdn_p if u < 2 else hg_p), (2, gdn_s if u < 2 else hg_s)):
                        pool.dma_start(out[0, 0, 2 * pair:2 * pair + 2].rearrange("h d v -> d h v"),
                                       S[:, part, :, :]).then_inc(state_out, 16)
                    if u + 1 < len(units):
                        pool.wait_ge(state_out, 32 * (u + 1))
                        load_state(u + 1)

        @block.scalar
        def _(act):
            walk = Walk(act)
            steps = [0]
            pend = []
            seen = dict(conv=0, og=0, val=0)

            def link(ins):
                steps[0] += 1
                ins.then_inc(act_step, 1)
                act.wait_ge(act_step, steps[0])

            def split_weights(i):
                if i >= len(jobs) or jobs[i].src == "c":
                    return
                m, job = nth_split[i], jobs[i]
                wait_weights(act, i, walk)
                if m >= 2:
                    act.wait_ge(job_done, walk.plus(split[m - 2] + 1, 4))
                act.activation(w_hi[:, m % 2, 0:job.nk, 0:job.m], raw[:, i % RAW, 0:job.nk, 0:job.m],
                               ACT.Copy).then_inc(w_hi_done, 1)

            def split_val(dst):
                v = seen["val"]
                seen["val"] += 1
                act.wait_ge(val_ready, v + 1)
                act.activation(dst, val[:, v % 2, :], ACT.Copy).then_inc(hi_ready, 1)

            def conv_silu():
                if not pend:
                    return
                dst = pend.pop()
                act.wait_ge(cy_ready, seen["conv"])
                act.activation(dst[:, 0:SEQ], cy[:, 0:SEQ], ACT.Silu)
                act.activation(dst[:, SEQ:TOK], cy[:, SMP:SMP + DEC], ACT.Silu).then_inc(conv_ready, 1)

            def rnorm(n, count):
                q, bank = norms[n], first_fill[n]
                dst = rn[:, q % 2, :]
                if q >= 2:
                    act.wait_ge(rn_used, q - 1)
                if count == D:
                    act.activation(warm[:, :], eps[:, :], ACT.Ln)
                for k, cols_ in enumerate(GROUPS):
                    act.wait_ge(fill_done, bank + k + 1)
                    act.activation(dst[:, cols_], R[:, (bank + k) % 4, 0:cols_.stop - cols_.start], ACT.Ln,
                                   bias=eps[:, 0:1], scale=1.0 / count).then_inc(bank_user["act"], 1)
                wait_bank(act, bank + 1)
                act.activation(dst, dst, ACT.Exp, scale=-0.5).then_inc(rn_ready, 1)

            def read_banks(n, k0, pieces, func=ACT.Copy, scale=1.0):
                for k, (dst, view) in enumerate(pieces):
                    act.wait_ge(fill_done, first_fill[n] + k0 + k + 1)
                    act.activation(dst, view((first_fill[n] + k0 + k) % 4), func, scale=scale)\
                        .then_inc(bank_user["act"], 1)

            def chunk_pieces(dst, square, feat=False):
                out = []
                for cs in FILLS:
                    L = length(cs[0])
                    d = dst[0:P if feat else L, cs[0]:cs[-1] + 1, :, 0:L if (square or feat) else P]
                    out.append((d, (lambda b, cs=cs: feat_view(b, cs)) if feat
                                else (lambda b, cs=cs: fill_view(b, cs, square))))
                return out

            act.dma_start(xtok[:, 0:N_CHUNK, :], t["x_prompt"].rearrange("b (c p) d -> p (b c) d", p=P)).then_inc(x_in, 16)
            act.dma_start(xtok[0:DEC, N_CHUNK, :], t["x_sample"].rearrange("b p d -> (b p) d")).then_inc(x_in, 16)
            act.wait_ge(eps_set, 1)
            for n, step in walk:
                name, a = step[0], step[1:]
                if name == "job":
                    split_weights(a[0] + 1)
                elif name == "vectors":
                    wait_bank(act, first_fill[n] + 1)
                    act.activation(cT[:, :, :], vT[:, NA + VB["c"]:NA + VB["c"] + 2 * KD]
                                   .rearrange("p (g k) -> p g k", g=2), ACT.Silu).then_inc(c_sig, 1)
                    act.activation(vec4[:, 2:3], vec4[:, 1:2], ACT.Exp).then_inc(sp_log, 1)
                elif name == "x_in":
                    read_banks(n, 0, [(xT[:, k, 0:SEQ], lambda b: R[:, b, 0:SEQ]) for k in range(KD)])
                    read_banks(n, KD, [(xT[:, :, SEQ:TOK], lambda b: R[:, b, 0:KD * DEC]
                                        .rearrange("p (k t) -> p k t", k=KD))])
                elif name in ("sums", "onorm", "g_norm"):
                    rnorm(n, dict(sums=D, onorm=P, g_norm=1)[name])
                elif name == "ada_q":
                    read_banks(n, 0, [(ada_rows[:, a[0] * 512:(a[0] + 1) * 512], lambda b: R[0:2, b, :])])
                elif name == "ada_T":
                    split_weights(0)
                elif name == "ogate":
                    split_val(o_hi[:, a[0], :])
                elif name == "h1":
                    for k in range(KD):
                        split_val(h_hi[:, k, :])
                elif name == "h2":
                    for k in range(KD):
                        v = seen["val"]
                        seen["val"] += 1
                        act.wait_ge(val_ready, v + 1)
                        for g, cols_ in enumerate(GROUPS):
                            ins = act.activation(h_hi[:, k, cols_], val[:, v % 2, cols_], ACT.Identity,
                                                 bias=mod[:, 3 * KD + k, g:g + 1])
                        ins.then_inc(hi_ready, 1)
                elif name == "g_sp":
                    act.wait_ge(x_rows, 1)
                    link(act.activation(rows[:, 1, :], rows[:, 1, :], ACT.Exp))
                    act.activation(rows[:, 1, :], rows[:, 1, :], ACT.Ln, bias=ones[0:NH, 0:1])
                    act.activation(rows[:, 2, :], rows[:, 2, :], ACT.Sigmoid).then_inc(sp_log, 1)
                elif name == "g_a":
                    act.wait_ge(sp_ready, 1)
                    act.activation(rows[:, 0, :], rows[:, 0, :], ACT.Exp, scale=vec4[:, 3:4]).then_inc(a_ready, 1)
                elif name == "g_sq":
                    conv_silu()
                elif name == "g_bcast":
                    read_banks(n, 0, [(abc[:, h, 0:SEQ], lambda b: R[:, b, 0:SEQ]) for h in range(2)])
                    read_banks(n, 2, [(abc[:, :, SEQ:TOK], lambda b: R[:, b, 0:2 * DEC]
                                       .rearrange("p (h t) -> p h t", h=2))])
                elif name in ("g_tok", "h_v"):
                    read_banks(n, 0, chunk_pieces(v_tok[:, a[0]], False))
                elif name == "g_x" and a[1]:
                    read_banks(n, 0, chunk_pieces(X, True)[:len(bank_users(step))])
                elif name == "g_w":
                    read_banks(n, 0, chunk_pieces(Wn, False, feat=True), scale=-1.0)
                elif name == "h_k":
                    read_banks(n, 0, chunk_pieces(kD, False))
                elif name in ("g_o", "h_o"):
                    h0 = (NH if name[0] == "g" else 0) + 2 * a[0]
                    c, L = a[1], length(a[1])
                    read_banks(n, 0, [(out_view(h0, c), lambda b: R[:, b, 0:2 * L].rearrange("p (h t) -> p h t", h=2))])
                elif name == "conv_out":
                    read_banks(n, 0, [(conv_rows[:, :], lambda b: R[0:72, b, 0:P])])
                elif name == "y_out":
                    read_banks(n, 0, [(ytok[0:length(c), c, j * 512:(j + 1) * 512], lambda b, c=c: R[0:length(c), b, :])
                                      for j in range(2) for c in range(CHUNKS)])
                elif name == "evac":
                    g = a[0]
                    kind, arg, _ = groups[g]
                    if kind == "conv":
                        what, pair, h, slot = arg
                        conv_silu()
                        c = seen["conv"]
                        seen["conv"] += 1
                        tile = dict(gq=0, gk=4, gv=8)[what] + 2 * pair + h
                        if c:
                            act.wait_ge(cy_ready, c)
                        else:
                            act.wait_ge(hist_zero, 1)
                        act.activation(ext[:, SEQ + 3:SEQ + 6], vT[:, NA + VB["conv_state"] + tile:
                                       NA + VB["conv_state"] + tile + 25:12], ACT.Copy)
                        wait_group(act, g)
                        s = g % 2
                        act.activation(ext[:, 3:3 + HALF], G[:, s, 0, 0:HALF], ACT.Copy)
                        act.activation(ext[:, 3 + HALF:3 + SEQ], G[:, s, 1, 0:SEQ - HALF], ACT.Copy)
                        act.activation(ext[:, SEQ + 6:EXT], G[:, s, 1, SEQ - HALF:HALF], ACT.Copy)\
                            .then_inc(slot_user["act"], 1)
                        wait_slot(act, g)
                        act.activation(conv_keep[:, 0, :, tile], ext[:, SEQ:SEQ + 3], ACT.Copy)
                        act.activation(conv_keep[:, 1, :, tile], ext[:, EXT - 3:EXT], ACT.Copy)\
                            .then_inc(ext_ready, 1)
                        pend.append(inp[:, pair, slot, :])
                    elif kind in ("hi", "hq"):
                        pair, h = arg
                        wait_group(act, g)
                        dst = inp[:, pair, (4 if kind == "hi" else 0) + h, :]
                        act.activation(halves(dst), slot_view(g), ACT.Copy,
                                       scale=QSCALE if kind == "hq" else 1.0).then_inc(slot_user["act"], 1)
                    elif kind == "hf":
                        pair, h = arg
                        wait_group(act, g)
                        act.activation(halves(inp[:, pair, 4 + h, :]), slot_view(g), ACT.Sigmoid)
                        act.activation(halves(inp[:, pair, 2 + h, :]), slot_view(g), ACT.Sigmoid, scale=-1.0)\
                            .then_inc(slot_user["act"], 1)
                    elif kind == "og":
                        if seen["og"] == 0:
                            wait_bank(act, last_bank[spot("g_o", 1, 3)])
                        seen["og"] += 1
                        wait_group(act, g)
                        act.activation(halves(o_gate[:, arg, :]), slot_view(g), ACT.Silu)\
                            .then_inc(slot_user["act"], 1)
                    elif kind == "gate":
                        k, m = (0, 1)[arg[0] == "b"], arg[1]
                        if m == 0:
                            act.wait_ge(conv_sent, 32)
                            act.wait_ge(state_out, 32 * len(units))
                        else:
                            wait_slot(act, groups_at[("pa", "pb")[k], m - 1])
                        wait_group(act, g)
                        act.activation(halves(gate[:, k, :]), slot_view(g), ACT.Sigmoid)\
                            .then_inc(slot_user["act"], 1)
                    elif kind == "pb":
                        if arg == 0:
                            act.wait_ge(state_out, 32 * len(units))
                        split_val(y_hi[:, arg, :])
                    elif kind == "ffg":
                        wait_group(act, g, walk)
                        if arg >= 2:
                            wait_slot(act, g - 3, walk)
                        act.activation(halves(g_act[:, arg % 2, :]), slot_view(g), ACT.Silu)\
                            .then_inc(slot_user["act"], 1)
                    elif kind == "ffu":
                        wait_slot(act, g, walk)
                        v = seen["val"] % 2
                        seen["val"] += 1
                        act.activation(a_hi[:, bass.ds(walk.plus(arg, 2), 1), :], val[:, v:v + 1, :], ACT.Copy)\
                            .then_inc(hi_ready, 1)

        @block.vector
        def _(dve):
            walk = Walk(dve)
            steps = [0]
            later = []
            seen = dict(val=0, conv=0, u=0, s=0)

            def link(ins):
                steps[0] += 1
                ins.then_inc(dve_step, 1)
                dve.wait_ge(dve_step, steps[0])

            def read(ins):
                ins.then_inc(bank_user["dve"], 1)

            def split_weights(i):
                if i >= len(jobs) or jobs[i].src == "c":
                    return
                m, job = nth_split[i], jobs[i]
                dve.wait_ge(w_hi_done, walk.plus(m + 1, 4))
                at = (slice(None), m % 2, slice(0, job.nk), slice(0, job.m))
                dve.tensor_tensor(w_lo[at], raw[:, i % RAW, 0:job.nk, 0:job.m], w_hi[at].bitcast(F32),
                                  ALU.subtract).then_inc(w_lo_done, 1)

            def low_parts(keep=0):
                while len(later) > keep:
                    v, hi, lo, shift = later.pop(0)
                    dve.wait_ge(hi_ready, walk.plus(v + 1, 2) if type(hi) is int else v + 1)
                    if type(hi) is int:
                        k = bass.ds(walk.plus(hi, 2), 1)
                        ins = dve.tensor_tensor(a_lo[:, k, :], val[:, v % 2:v % 2 + 1, :], a_hi[:, k, :].bitcast(F32),
                                                ALU.subtract)
                    elif shift is None:
                        ins = dve.tensor_tensor(lo, val[:, v % 2, :], hi.bitcast(F32), ALU.subtract)
                    else:
                        for g, cols_ in enumerate(GROUPS):
                            ins = dve.scalar_tensor_tensor(lo[:, cols_], val[:, v % 2, cols_], shift[:, g:g + 1],
                                                           hi[:, cols_].bitcast(F32), ALU.add, ALU.subtract)
                    ins.then_inc(lo_ready, 1)

            def new_val(hi, lo, shift=None):
                v = seen["val"]
                seen["val"] += 1
                low_parts(1)
                if v >= 2:
                    dve.wait_ge(lo_ready, walk.plus(v - 1, 2))
                later.append((v, hi, lo, shift))
                return val[:, v % 2, :]

            def rnorm(n):
                dve.wait_ge(rn_ready, norms[n] + 1)
                return rn[:, norms[n] % 2, :]

            def bank(n, k):
                dve.wait_ge(fill_done, first_fill[n] + k + 1)
                return (first_fill[n] + k) % 4

            def add_square(m):
                if m == 0:
                    link(dve.tensor_tensor(acc[:, :], xT[:, 0, :], xT[:, 0, :], ALU.mult))
                else:
                    link(dve.tensor_tensor(sq[:, 0, :], xT[:, m, :], xT[:, m, :], ALU.mult))
                    ins = dve.tensor_tensor(acc[:, :], acc[:, :], sq[:, 0, :], ALU.add)
                    if m == KD - 1:
                        ins.then_inc(acc_ready, 1)
                    else:
                        link(ins)

            dve.memset(eps[:, :], EPS).then_inc(eps_set, 1)
            for n, step in walk:
                name, a = step[0], step[1:]
                if n == up[2]:
                    seen["val"] += 2 * walk.passed
                    later[:] = [(v + 2 * walk.passed, k + 2 * walk.passed, *z) for v, k, *z in later]
                if name == "job":
                    split_weights(a[0] + 1)
                    low_parts()
                elif name == "vectors":
                    b = bank(n, 0)
                    read(dve.tensor_copy(vT[:, 0:NA], R[:, b, 0:NA]))
                    b = bank(n, 1)
                    read(dve.tensor_copy(vT[:, NA:NA + NB], R[:, b, 0:NB]))
                    wait_bank(dve, first_fill[n] + 1)
                elif name == "x_in" and order[n] == 0:
                    wait_bank(dve, first_fill[n] + KD)
                    for k in range(KD):
                        add_square(k)
                elif name == "sums":
                    mean_rn = rnorm(n)
                elif name == "x_norm":
                    for k in range(KD):
                        ins = dve.tensor_tensor(xT[:, k, :], xT[:, k, :], mean_rn, ALU.mult)
                    ins.then_inc(rn_used, 1)
                    dve.wait_ge(rn_used, norms[n])
                elif name == "ada_T":
                    split_weights(0)
                    b = bank(n, 0)
                    read(dve.tensor_tensor(mod[:, 0:2 * KD, :], R[:, b, 0:4 * KD].rearrange("p (k g) -> p k g", g=2),
                                           bc(vT[:, 0:2 * KD], 2), ALU.add))
                    wait_bank(dve, first_fill[n])
                    dve.memset(ext[:, 0:3], 0.0).then_inc(hist_zero, 1)
                elif name in ("h1", "h2"):
                    low_parts()
                    sh, sc, norm = (0, 1, "norm_mix") if name == "h1" else (3, 4, "norm_ffn")
                    for g in range(2):
                        ins = dve.scalar_tensor_tensor(gain[:, g, :], mod[:, sc * KD:(sc + 1) * KD, g], 1.0,
                                                       vT[:, NA + VB[norm]:NA + VB[norm] + KD], ALU.add, ALU.mult)
                    link(ins)
                    for k in range(KD):
                        x = new_val(h_hi[:, k, :], h_lo[:, k, :], None if name == "h1" else mod[:, sh * KD + k, :])
                        for g, cols_ in enumerate(GROUPS):
                            if name == "h1":
                                ins = dve.tensor_scalar(x[:, cols_], xT[:, k, cols_], gain[:, g, k:k + 1],
                                                        mod[:, sh * KD + k, g:g + 1], ALU.mult, ALU.add)
                            else:
                                ins = dve.scalar_tensor_tensor(x[:, cols_], xT[:, k, cols_], gain[:, g, k:k + 1],
                                                               mean_rn[:, cols_], ALU.mult, ALU.mult)
                        ins.then_inc(val_ready, 1)
                        low_parts(1)
                    low_parts()
                elif name == "g_a":
                    dve.wait_ge(sp_log, 2)
                    dve.tensor_tensor(rows[:, 0, :], rows[:, 0, :], rows[:, 1, :], ALU.add).then_inc(sp_ready, 1)
                elif name == "g_scan":
                    dve.wait_ge(a_ready, 1)
                    for c in range(CHUNKS):
                        ins = dve.tensor_tensor_scan(rows[:, 3, toks(c)], rows[:, 0, toks(c)],
                                                     ones[0:NH, 0:length(c)], 1.0, ALU.mult, ALU.mult)
                    ins.then_inc(pg_ready, 1)
                elif name == "g_rows":
                    b = bank(n, 0)
                    for c0, c1, L in ((0, N_CHUNK, P), (N_CHUNK, CHUNKS, DEC)):
                        ins = dve.tensor_copy(cols[0:L, c0:c1, :, :].rearrange("p c k h -> p c (k h)"),
                                              R[0:L, b, 8 * c0:8 * c1].rearrange("p (c k) -> p c k", c=c1 - c0))
                    read(ins)
                    wait_bank(dve, first_fill[n])
                elif name == "g_sq":
                    dve.wait_ge(conv_ready, 6 * (a[0] + 1))
                    for k in range(2):
                        x = inp[:, a[0], k, :]
                        dve.tensor_tensor(sq[:, (head_norms[n] + k) % 2, :], x, x, ALU.mult).then_inc(sq_ready, 1)
                elif name == "g_norm":
                    pair, k = a
                    x = inp[:, pair, k, :]
                    r_ = rnorm(n)
                    dve.scalar_tensor_tensor(x, x, QSCALE if k < 2 else 1.0, r_, ALU.mult, ALU.mult)\
                        .then_inc(rn_used, 1)
                    if k + 2 < 4:
                        x = inp[:, pair, k + 2, :]
                        dve.tensor_tensor(sq[:, head_norms[n] % 2, :], x, x, ALU.mult).then_inc(sq_ready, 1)
                elif name == "g_gram":
                    pair = a[0]
                    wait_bank(dve, last_bank[spot("g_bcast", pair)])
                    for c in range(CHUNKS):
                        L = length(c)
                        for h in range(2):
                            ins = dve.tensor_tensor_scan(relT[0:L, c, h, 0:L], abc[0:L, h, toks(c)],
                                                         ident[0:L, 0:L], 0.0, ALU.mult, ALU.add)
                    link(ins)
                    for k, cs in enumerate(FILLS):
                        b = bank(n, k)
                        L = length(cs[0])
                        for c in cs:
                            for h in range(2):
                                ins = dve.scalar_tensor_tensor(N[0:L, c, h, 0:L], relT[0:L, c, h, 0:L],
                                                               cols[0:L, c, 0, 2 * pair + h:2 * pair + h + 1],
                                                               fill_view(b, cs)[:, c - cs[0], h, :],
                                                               ALU.mult, ALU.mult)
                        read(ins)
                    for k, cs in enumerate(FILLS):
                        b = bank(n, 3 + k)
                        L = length(cs[0])
                        d = (slice(0, L), slice(cs[0], cs[-1] + 1), slice(None), slice(0, L))
                        read(dve.tensor_tensor(PT[d], relT[d], fill_view(b, cs), ALU.mult))
                elif name == "g_tok":
                    pair = a[0]
                    hs = slice(2 * pair, 2 * pair + 2)
                    for k, cs in enumerate(FILLS):
                        b = bank(n, 3 + k)
                        L, cc = length(cs[0]), slice(cs[0], cs[-1] + 1)
                        for i, c in enumerate(cs):
                            dve.tensor_tensor(kPG[0:L, c, :, :], fill_view(b, cs, False)[:, i], bc(cols[0:L, c, 1, hs], P),
                                              ALU.mult)
                            ins = dve.tensor_tensor(kD[0:L, c, :, :], fill_view(b, cs, False)[:, i],
                                                    bc(relT[0:L, c, :, L - 1], P), ALU.mult)
                        read(ins)
                    q = inp[:, pair, 0:2, :]
                    for h in range(2):
                        b = bank(n, 6 + h)
                        dve.tensor_copy(elast[:, 0:N_CHUNK, h], R[:, b, P - 1:SEQ:P])
                        read(dve.tensor_tensor(q[:, h, 0:SEQ], q[:, h, 0:SEQ], R[:, b, 0:SEQ], ALU.mult))
                    b = bank(n, 8)
                    v = R[:, b, 0:2 * DEC].rearrange("p (h t) -> p h t", h=2)
                    dve.tensor_copy(elast[:, N_CHUNK, :], v[:, :, DEC - 1])
                    read(dve.tensor_tensor(q[:, :, SEQ:TOK], q[:, :, SEQ:TOK], v, ALU.mult))
                elif name == "g_x" and a[1] == 0:
                    for k, cs in enumerate(FILLS):
                        b = bank(n, k)
                        L = length(cs[0])
                        m = 2 * len(cs)
                        read(dve.tensor_tensor(joined(Tm, cs), mid(ident[0:L, 0:L], m),
                                               R[0:L, b, 0:m * L].rearrange("p (m t) -> p m t", m=m), ALU.subtract))
                elif name == "g_y":
                    pair, lv = a
                    todo = FILLS if lv < 5 else FILLS[:2]
                    k = 0
                    if lv == 1:
                        dve.wait_ge(U0_ready, pair + 1)
                    wait_bank(dve, last_bank[spot("g_x", pair, 0) if lv == 1 else spot("g_y", pair, lv - 1)])
                    for cs in todo:
                        for dst in ((Tm, Um) if lv < LEVELS - 1 else (Um,)):
                            b = bank(n, k)
                            L = length(cs[0])
                            d = (slice(0, L), slice(cs[0], cs[-1] + 1), slice(None), slice(0, L))
                            read(dve.tensor_tensor(dst[d], dst[d], fill_view(b, cs), ALU.subtract))
                            k += 1
                elif name == "g_u":
                    pair, c = a
                    L = length(c)
                    b = bank(n, 0)
                    if seen["u"]:
                        dve.wait_ge(fill_done, last_bank[max(i for i in range(n) if plan[i][0] == "g_o")] + 1)
                    seen["u"] += 1
                    read(dve.tensor_tensor(u_tok[0:L, :, :], R[0:L, b, 0:2 * P].rearrange("p (h v) -> p h v", h=2),
                                           bc(cols[0:L, c, 0, 2 * pair:2 * pair + 2], P), ALU.mult))
                elif name in ("g_o", "h_o"):
                    pair, c = a
                    u = unit(name, pair)
                    b = bank(n, 1)
                    if seen["s"] % CHUNKS == 0 and u:
                        dve.wait_ge(state_out, 32 * u)
                    if c == N_CHUNK:
                        dve.wait_ge(state_in, 16 * (u + 1))
                    if seen["s"]:
                        wait_bank(dve, last_state(n))
                    old, new = (2, 2) if c == N_CHUNK else (c % 2, (c + 1) % 2)
                    for h in range(2):
                        new_s = R[:, b, h * P:(h + 1) * P]
                        if c == 0:
                            ins = dve.tensor_copy(S[:, new, h, :], new_s)
                        else:
                            last = (c + 1) * P - 1 if c < N_CHUNK else TOK - 1
                            decay = elast[:, c, h:h + 1] if name == "g_o" else inp[:, pair, 4 + h, last:last + 1]
                            ins = dve.scalar_tensor_tensor(S[:, new, h, :], S[:, old, h, :], decay, new_s,
                                                           ALU.mult, ALU.add)
                    read(ins)
                    seen["s"] += 1
                elif name == "h_diag":
                    dve.wait_ge(at_zero, a[0] + 1)
                    copy_scores(dve, read, bank, n, LEVELS)
                    q, f = inp[:, a[0], 0:2, :], inp[:, a[0], 4:6, :]
                    dve.wait_ge(slot_user["act"], slot_freed[max(g for g, x in enumerate(groups)
                                                             if x[0] == "hf" and x[1] == (a[0], 1))][1])
                    dve.tensor_tensor(q, q, f, ALU.mult).then_inc(hg_ready, 1)
                elif name == "h_level":
                    pair, lv = a
                    copy_scores(dve, read, bank, n, lv)
                    h = 1 << lv
                    end = TOK if lv < 5 else SEQ
                    q, k, f = (inp[:, pair, s:s + 2, 0:end].rearrange("p n (b x t) -> p n b x t", x=2, t=h)
                               for s in (0, 2, 4))
                    dve.wait_ge(hg_ready, order[n] + pair + 1)
                    for hd in range(2):
                        dve.tensor_tensor(q[:, hd, :, 1, :], q[:, hd, :, 1, :], bc(f[:, hd, :, 0, h - 1], h), ALU.mult)
                        ins = dve.tensor_tensor(k[:, hd, :, 0, :], k[:, hd, :, 0, :], bc(f[:, hd, :, 1, h - 1], h), ALU.mult)
                    link(ins)
                    dve.tensor_tensor(f[:, :, :, 1, h - 1], f[:, :, :, 1, h - 1], f[:, :, :, 0, h - 1],
                                      ALU.mult).then_inc(hg_ready, 1)
                elif name == "o_sq":
                    hd = a[0]
                    h = head_norms[n] + sum(s[0] == "o_sq" for s in plan[:n]) - sum(s[0] == "onorm" for s in plan[:n])
                    wait_bank(dve, last_bank[spot("h_o" if hd < NH else "g_o", hd % NH // 2, 3)] - 1)
                    dve.tensor_tensor(sq[:, h % 2, :], o[:, hd, :], o[:, hd, :], ALU.mult).then_inc(sq_ready, 1)
                elif name == "onorm":
                    hd = a[0]
                    w = NA + (VB["hg"] if hd < NH else VB["gdn"])
                    dve.scalar_tensor_tensor(o[:, hd, :], o[:, hd, :], vT[:, w:w + 1], rnorm(n),
                                             ALU.mult, ALU.mult).then_inc(rn_used, 1)
                elif name == "ogate":
                    hd = a[0]
                    if hd == 0:
                        dve.wait_ge(conv_sent, 32)
                        dve.wait_ge(rn_used, norms[n])
                    x = new_val(o_hi[:, hd, :], o_lo[:, hd, :])
                    wait_slot(dve, groups_at["og", hd])
                    dve.tensor_tensor(x, o[:, hd, :], o_gate[:, hd, :], ALU.mult).then_inc(val_ready, 1)
                    low_parts(1)
                elif name == "y_out":
                    for k in range(KD):
                        dve.scalar_tensor_tensor(xT[:, k, :], xT[:, k, :], vT[:, NA + VB["final"] + k:NA + VB["final"] + k + 1],
                                                 mean_rn, ALU.mult, ALU.mult).then_inc(yT_ready, 1)
                elif name == "evac":
                    g = a[0]
                    kind, arg, _ = groups[g]
                    s = g % 2
                    done = slot_user["dve"]
                    if kind == "ada":
                        wait_group(dve, g)
                        c = arg[0] * KD + arg[1]
                        dve.tensor_scalar(mod[:, c, :], G[:, s, 0, 0:2], vT[:, c:c + 1], None, ALU.add)\
                            .then_inc(done, 1)
                    elif kind == "gagb":
                        wait_group(dve, g)
                        dve.wait_ge(sp_log, 1)
                        dve.tensor_scalar(vec4[:, 3:4], vec4[:, 2:3], -1.0, None, ALU.mult)
                        ga = G[0:NH, s, :, 0:HALF]
                        dve.tensor_scalar(halves(rows[:, 0, :]), ga, vec4[:, 0:1], 0.0, ALU.add, ALU.max)
                        dve.tensor_copy(halves(rows[:, 2, :]), G[32:32 + NH, s, :, 0:HALF])
                        dve.tensor_scalar(halves(rows[:, 1, :]), ga, vec4[:, 0:1], None, ALU.add).then_inc(done, 1)
                        wait_slot(dve, g)
                        dve.scalar_tensor_tensor(rows[:, 1, :], rows[:, 0, :], -2.0, rows[:, 1, :], ALU.mult,
                                                 ALU.add).then_inc(x_rows, 1)
                    elif kind == "conv":
                        what, pair, h, slot = arg
                        c = seen["conv"]
                        seen["conv"] += 1
                        tile = dict(gq=0, gk=4, gv=8)[what] + 2 * pair + h
                        dve.wait_ge(ext_ready, c + 1)
                        if c:
                            dve.wait_ge(conv_ready, c)
                        w = [vT[:, 48 + j * 12 + tile:49 + j * 12 + tile] for j in range(CONV_W)]
                        link(dve.tensor_scalar(cy[:, :], ext[:, 0:CO], w[0], None, ALU.mult))
                        for j in range(1, CONV_W):
                            ins = dve.scalar_tensor_tensor(cy[:, :], ext[:, j:j + CO], w[j], cy[:, :], ALU.mult, ALU.add)
                            if j < CONV_W - 1:
                                link(ins)
                        ins.then_inc(cy_ready, 1)
                    elif kind in ("pa", "pb"):
                        wait_group(dve, g)
                        k = 0 if kind == "pa" else 1
                        wait_slot(dve, groups_at["gate", ("ab"[k], arg)])
                        if arg == 0:
                            dve.wait_ge(state_out, 32 * len(units))
                        dve.tensor_tensor(halves(ya[:, k, :]), slot_view(g), halves(gate[:, k, :]), ALU.mult)\
                            .then_inc(done, 1)
                        wait_slot(dve, g)
                        if kind == "pb":
                            x = new_val(y_hi[:, arg, :], y_lo[:, arg, :])
                            dve.tensor_tensor(x, ya[:, 0, :], ya[:, 1, :], ALU.add).then_inc(val_ready, 1)
                    elif kind in ("out", "down"):
                        wait_group(dve, g)
                        v = 2 if kind == "out" else 5
                        if kind == "out" and arg == 0:
                            wait_bank(dve, last_bank[len(plan) - 1 - plan[::-1].index(("x_in",))])
                        for grp, half, inside, cols_ in PIECES:
                            ins = dve.scalar_tensor_tensor(xT[:, arg, cols_], G[:, s, half, inside],
                                                           mod[:, v * KD + arg, grp:grp + 1], xT[:, arg, cols_],
                                                           ALU.mult, ALU.add)
                        ins.then_inc(done, 1)
                        wait_slot(dve, g)
                        add_square(arg)
                    elif kind == "ffu":
                        wait_group(dve, g, walk)
                        wait_slot(dve, g - 1, walk)
                        x = new_val(arg, None)
                        dve.tensor_tensor(halves(x), slot_view(g), halves(g_act[:, arg % 2, :]), ALU.mult)\
                            .then_inc(done, 1)

        @block.tensor
        def _(pe):
            walk = Walk(pe)
            seen = dict(s=0, lo=0)

            def fill(n, k, products):
                f = first_fill[n] + k
                if f >= 4:
                    wait_bank(pe, f - 4)
                for make in products:
                    ins = make(f % 4)
                ins.then_inc(fill_done, 1)

            def products(i, half):
                job, m = jobs[i], nth_split[i]
                hi, lo = src[job.src]
                cols_ = slice(half * HALF, (half + 1) * HALF)
                out = G[0:job.m, job.group % 2, half, 0:HALF]
                for k in range(job.nk):
                    need = vals_before[job.src] + job.k0 + k + 1
                    if need > seen["lo"]:
                        pe.wait_ge(lo_ready, need)
                        seen["lo"] = need
                    wh, wl = (w[:, m % 2, k, 0:job.m] for w in (w_hi, w_lo))
                    xh, xl = (x[:, job.k0 + k, cols_] for x in (hi, lo))
                    for p, (w, x) in enumerate(((wh, xh), (wh, xl), (wl, xh))):
                        ins = pe.matmul(out, w, x, start=(job.first and k == 0 and p == 0),
                                        stop=(job.last and k == job.nk - 1 and p == 2))
                return ins

            def mm(out, lhsT, rhs, start=True, stop=True):
                return lambda b: pe.matmul(out(b), lhsT, rhs, start=start, stop=stop, skip_group_check=True)

            def tr(out, in_):
                return lambda b: pe.transpose(out(b), in_, ident[0:in_.shape[0], 0:in_.shape[0]])

            def each(cs):
                return [(i, c, h) for i, c in enumerate(cs) for h in range(2)]

            def sums_of(n, k, x):
                fill(n, k, [mm(lambda b: R[:, b, 0:SEQ], ones[:, :], x[:, 0:SEQ])])
                fill(n, k + 1, [mm(lambda b: R[:, b, 0:DEC], ones[:, :], x[:, SEQ:TOK])])

            def wait_lv(pair, lv):
                if lv == 0:
                    wait_bank(pe, last_bank[spot("g_x", pair, 0)])
                    pe.wait_ge(U0_ready, pair + 1)
                else:
                    wait_bank(pe, last_bank[spot("g_y", pair, lv)])

            pe.wait_ge(const_in, 48)
            for n, step in walk:
                name, a = step[0], step[1:]
                if name == "job":
                    i = a[0]
                    job = jobs[i]
                    g = job.group
                    if job.first and g >= 2:
                        wait_slot(pe, g - 2, walk)
                    if job.src == "c":
                        wait_weights(pe, i, walk)
                        pe.wait_ge(c_sig, 1)
                        for k in range(KD):
                            ins = pe.matmul(G[:, g % 2, 0, 0:2], raw[:, i % RAW, k, :], cT[:, :, k],
                                            start=(k == 0), stop=(k == KD - 1), skip_group_check=True)
                        ins.then_inc(job_done, 1)
                    else:
                        pe.wait_ge(w_lo_done, walk.plus(nth_split[i] + 1, 4))
                        products(i, 0)
                elif name == "half":
                    products(a[0], 1).then_inc(job_done, 1)
                elif name == "vectors":
                    pe.wait_ge(vec_in, 16 * 12)
                    fill(n, 0, [tr(lambda b: R[:, b, 0:NA], vecs[0:NA, 0, :])])
                    fill(n, 1, [tr(lambda b: R[:, b, 0:NB], vecs[0:NB, 1, :])])
                elif name == "x_in":
                    pe.wait_ge(x_in, 32 * (order[n] + 1))
                    for k in range(KD):
                        fill(n, k, [tr(lambda b, c=c: R[:, b, c * P:(c + 1) * P], xtok[:, c, k * P:(k + 1) * P])
                                    for c in range(N_CHUNK)])
                    fill(n, KD, [tr(lambda b, k=k: R[:, b, k * DEC:(k + 1) * DEC],
                                    xtok[0:DEC, N_CHUNK, k * P:(k + 1) * P]) for k in range(KD)])
                elif name == "ada_q":
                    pe.wait_ge(c_sig, 1)
                    pe.wait_ge(ada_in[a[0]], 16)
                    fill(n, 0, [mm(lambda b, k=k: R[0:2, b, :], cT[:, :, k], wada01[:, k, a[0] * 512:(a[0] + 1) * 512],
                                   k == 0, k == KD - 1) for k in range(KD)])
                elif name == "ada_T":
                    wait_bank(pe, first_fill[n] - 1)
                    fill(n, 0, [tr(lambda b, m=m: R[:, b, 2 * m:2 * m + 2], ada_rows[:, m * P:(m + 1) * P])
                                for m in range(2 * KD)])
                elif name == "sums":
                    pe.wait_ge(acc_ready, order[n] + 1)
                    sums_of(n, 0, acc[:, :])
                elif name in ("g_norm", "onorm"):
                    pe.wait_ge(sq_ready, head_norms[n] + 1)
                    sums_of(n, 0, sq[:, head_norms[n] % 2, :])
                elif name == "g_rows":
                    pe.wait_ge(pg_ready, 1)
                    fill(n, 0, [tr(lambda b, c=c, j=j: R[0:length(c), b, c * 8 + 4 * j:c * 8 + 4 * j + 4],
                                   rows[:, (2, 3)[j], toks(c)]) for c in range(CHUNKS) for j in range(2)])
                elif name == "g_bcast":
                    pair = a[0]
                    for h in range(2):
                        fill(n, h, [mm(lambda b: R[:, b, 0:SEQ], sel[:, 2 * pair + h, :], rows[:, 0, 0:SEQ])])
                    fill(n, 2, [mm(lambda b, h=h: R[:, b, h * DEC:(h + 1) * DEC], sel[:, 2 * pair + h, :],
                                   rows[:, 0, SEQ:TOK]) for h in range(2)])
                elif name == "g_gram":
                    pair = a[0]
                    pe.wait_ge(rn_used, norms[spot("g_norm", pair, 3)] + 1)
                    q, k_ = inp[:, pair, 0:2, :], inp[:, pair, 2:4, :]
                    for j, y in enumerate((k_, q)):
                        for k, cs in enumerate(FILLS):
                            fill(n, 3 * j + k, [mm(lambda b, i=i, h=h, cs=cs: fill_view(b, cs)[:, i, h, :],
                                                   k_[:, h, toks(c)], y[:, h, toks(c)]) for i, c, h in each(cs)])
                elif name in ("g_tok", "h_v"):
                    pair = a[0]
                    if name == "h_v":
                        wait_slot(pe, max(g for g, z in enumerate(groups) if z[0] == "hi" and z[1] == (pair, 1)))
                    for j, s in enumerate((4, 2) if name == "g_tok" else (4,)):
                        for k, cs in enumerate(FILLS):
                            fill(n, 3 * j + k, [tr(lambda b, i=i, h=h, cs=cs: fill_view(b, cs, False)[:, i, h, :],
                                                   inp[:, pair, s + h, toks(c)]) for i, c, h in each(cs)])
                    if name == "g_tok":
                        for h in range(2):
                            fill(n, 6 + h, [mm(lambda b: R[:, b, 0:SEQ], sel[:, 2 * pair + h, :], rows[:, 3, 0:SEQ])])
                        fill(n, 8, [mm(lambda b, h=h: R[:, b, h * DEC:(h + 1) * DEC], sel[:, 2 * pair + h, :],
                                       rows[:, 3, SEQ:TOK]) for h in range(2)])
                elif name == "g_x":
                    pair, lv = a
                    pe.wait_ge(Nl_ready, order[n] + 1)
                    for k, cs in enumerate(FILLS if lv < 5 else FILLS[:2]):
                        if lv == 1:
                            wait_bank(pe, first_fill[spot("g_x", pair, 0)] + k)
                        elif lv:
                            wait_bank(pe, first_fill[spot("g_y", pair, lv - 1)] + 2 * k)
                        fill(n, k, [mm(lambda b, i=i, h=h, cs=cs: fill_view(b, cs)[:, i, h, :],
                                       Nl[0:length(c), c, h, 0:length(c)],
                                       Tm[0:length(c), c, h, 0:length(c)] if lv else
                                       ident[0:length(c), 0:length(c)]) for i, c, h in each(cs)])
                elif name == "g_y":
                    pair, lv = a
                    if lv == 1:
                        pe.wait_ge(U0_ready, pair + 1)
                    else:
                        wait_bank(pe, last_bank[spot("g_y", pair, lv - 1)])
                    k = 0
                    for j, cs in enumerate(FILLS if lv < 5 else FILLS[:2]):
                        wait_bank(pe, first_fill[spot("g_x", pair, lv)] + j)
                        for l_, r_ in (((Um, X), (X, Um)) if lv < LEVELS - 1 else ((X, Um),)):
                            fill(n, k, [mm(lambda b, i=i, h=h, cs=cs: fill_view(b, cs)[:, i, h, :],
                                           l_[0:length(c), c, h, 0:length(c)], r_[0:length(c), c, h, 0:length(c)])
                                        for i, c, h in each(cs)])
                            k += 1
                elif name == "g_w":
                    pair = a[0]
                    wait_lv(pair, LEVELS - 1)
                    wait_bank(pe, first_fill[spot("g_tok", pair)] + 5)
                    for k, cs in enumerate(FILLS):
                        fill(n, k, [mm(lambda b, i=i, h=h, cs=cs: feat_view(b, cs)[:, i, h, :],
                                       kPG[0:length(c), c, h, :], Um[0:length(c), c, h, 0:length(c)])
                                    for i, c, h in each(cs)])
                elif name == "g_u":
                    pair, c = a
                    L = length(c)
                    u = unit(name, pair)
                    wait_bank(pe, last_bank[spot("g_w", pair)])
                    wait_bank(pe, last_bank[spot("g_tok", pair)])
                    if c == N_CHUNK:
                        pe.wait_ge(state_in, 16 * (u + 1))
                    if seen["s"]:
                        wait_bank(pe, last_state(n))
                    s_at = 2 if c == N_CHUNK else c % 2
                    make = []
                    for h in range(2):
                        out = (lambda b, h=h: R[0:L, b, h * P:(h + 1) * P])
                        make.append(mm(out, Um[0:L, c, h, 0:L], v_tok[0:L, pair, c, h, :], True, c == 0))
                        if c:
                            make.append(mm(out, Wn[:, c, h, 0:L], S[:, s_at, h, :], False, True))
                    fill(n, 0, make)
                elif name in ("g_o", "h_o"):
                    pair, c = a
                    L = length(c)
                    u = unit(name, pair)
                    s_at = 2 if c == N_CHUNK else c % 2
                    if name == "g_o":
                        wait_bank(pe, first_fill[n] - 1)
                        kt, vt, sc = kD, (lambda h: u_tok[0:L, h, :]), PT
                    else:
                        wait_bank(pe, last_bank[spot("h_k", pair)])
                        if c == N_CHUNK:
                            pe.wait_ge(state_in, 16 * (u + 1))
                        wait_bank(pe, last_state(n))
                        kt, vt, sc = kD, (lambda h: v_tok[0:L, pair, c, h, :]), PT
                    seen["s"] += 1
                    make = []
                    for h in range(2):
                        out = (lambda b, h=h: R[:, b, h * L:(h + 1) * L])
                        make.append(mm(out, vt(h), sc[0:L, c, h, 0:L], True, c == 0))
                        if c:
                            make.append(mm(out, S[:, s_at, h, :], inp[:, pair, h, toks(c)], False, True))
                    fill(n, 0, make)
                    fill(n, 1, [mm(lambda b, h=h: R[:, b, h * P:(h + 1) * P], kt[0:L, c, h, :], vt(h))
                                for h in range(2)])
                elif name in ("h_diag", "h_level"):
                    pair = a[0]
                    if name == "h_diag":
                        wait_slot(pe, max(g for g, z in enumerate(groups) if z[0] == "hf" and z[1] == (pair, 1)))
                        todo = FILLS
                    else:
                        pe.wait_ge(hg_ready, order[n] + pair + 1)
                        todo = FILLS if a[1] < 5 else FILLS[:2]
                    for k, cs in enumerate(todo):
                        fill(n, k, [mm(lambda b, i=i, h=h, cs=cs: fill_view(b, cs)[:, i, h, :],
                                       inp[:, pair, 2 + h, toks(c)], inp[:, pair, h, toks(c)]) for i, c, h in each(cs)])
                elif name == "h_k":
                    pair = a[0]
                    pe.wait_ge(hg_ready, (LEVELS + 1) * (pair + 1))
                    for k, cs in enumerate(FILLS):
                        fill(n, k, [tr(lambda b, i=i, h=h, cs=cs: fill_view(b, cs, False)[:, i, h, :],
                                       inp[:, pair, 2 + h, toks(c)]) for i, c, h in each(cs)])
                elif name == "conv_out":
                    pe.wait_ge(ext_ready, 12)
                    fill(n, 0, [tr(lambda b: R[0:72, b, 0:P], conv_keep[:, :, :, :].rearrange("p g j n -> p (g j n)"))])
                elif name == "y_out":
                    def out_tile(k, c):
                        def make(b):
                            pe.wait_ge(yT_ready, k + 1)
                            return tr(lambda b: R[0:length(c), b, k % 4 * P:(k % 4 + 1) * P], xT[:, k, toks(c)])(b)
                        return make

                    for j in range(2):
                        for c in range(CHUNKS):
                            fill(n, CHUNKS * j + c, [out_tile(4 * j + k, c) for k in range(4)])


_INS = ["x_prompt", "x_sample", "state_hgrn", "state_gdn", "state_conv", "c_prompt", "c_sample", "w_ada",
        "b_ada", "norm_mix", "w_in", "hg_lb", "hg_norm", "conv_w", "gdn_a_log", "gdn_dt_bias", "gdn_norm",
        "w_proj_a", "w_proj_b", "w_out", "norm_ffn", "w_up", "w_down", "final_norm"]
_OUTS = [(1, SEQ, D), (1, DEC, D), (1, 1, NH, P, P), (1, 1, NH, P, P), (1, 1, CONV_W - 1, 12 * P),
         (1, 1, NH, P, P), (1, 1, NH, P, P), (1, 1, CONV_W - 1, 12 * P)]


def constants():
    s, tt = np.arange(P)[:, None], np.arange(P)[None, :]
    levels = [((s >> lv) % 2 == 0) & ((tt >> lv) % 2 == 1) & (s >> (lv + 1) == tt >> (lv + 1))
              for lv in range(LEVELS)] + [s == tt]
    select = np.zeros((NH, NH, P), np.float32)
    for h in range(NH):
        select[h, h] = 1
    return {"level_masks": np.stack(levels, 1).astype(np.float32), "all_ones": np.ones((P, P), np.float32),
            "head_select": select}


def kernel(**inputs):
    import concourse.bacc as _bacc
    from concourse.bass_utils import run_bass_kernel_spmd as _run

    nc = _bacc.Bacc("TRN2", target_bir_lowering=False, num_devices=1)
    arrays, t = {}, {}
    for name, value in [*((n, inputs[n]) for n in _INS), *constants().items()]:
        a = np.ascontiguousarray(value)
        arrays[f"in_{name}"] = a
        t[name] = nc.dram_tensor(f"in_{name}", a.shape, mybir.dt.from_np(a.dtype), kind="ExternalInput").ap()
    for name, short in (("w_ada", "w_ada"), ("w_in", "w_in"), ("w_proj_a", "w_pa"), ("w_proj_b", "w_pb"),
                        ("w_out", "w_out"), ("w_up", "w_up"), ("w_down", "w_down")):
        t[short] = t[name][0]
    outs = [nc.dram_tensor(f"out_{i}", shape, F32, kind="ExternalOutput").ap() for i, shape in enumerate(_OUTS)]
    build(nc, t, outs)
    r = _run(nc, [arrays], core_ids=[0])
    return tuple(r.results[0][f"out_{i}"] for i in range(len(_OUTS)))
```
